# Optimizing a Trainium2 kernel written in Bass

```python
import math
import jax, jax.numpy as jnp
from jax import lax
import numpy as np

D_MODEL = 1024
BATCH = 1
SEQ = 512
DEPTH = 2

RET_HEADS = 4
RET_DK = 64
RET_DV = 128
RET_THETA = 10000.0
ATT_HEADS = 4
ATT_DIM = 64
ROPE_THETA = 500000.0
ROPE_DIMS = ATT_DIM // 4
DILATED_BRANCHES = ((128, 1), (512, 4), (2048, 16))
ATT_BLOCK = 128
MLSTM_HEADS = 4
MLSTM_DIM = 64
CONV_WIDTH = 4
CHUNK = 128
MIX_WIDTH = RET_HEADS * RET_DV + ATT_HEADS * ATT_DIM + MLSTM_HEADS * MLSTM_DIM
IN_SPLITS = (RET_HEADS * RET_DK, RET_HEADS * RET_DK, RET_HEADS * RET_DV, RET_HEADS * RET_DV,
             ATT_HEADS * ATT_DIM, ATT_HEADS * ATT_DIM, ATT_HEADS * ATT_DIM,
             MLSTM_HEADS * MLSTM_DIM, MLSTM_HEADS * MLSTM_DIM, MLSTM_HEADS * MLSTM_DIM,
             MLSTM_HEADS * MLSTM_DIM, MLSTM_HEADS, MLSTM_HEADS)
W_IN_COLS = sum(IN_SPLITS)
PEER_HEADS = 8
PEER_NKEYS = 128
PEER_EXPERTS = PEER_NKEYS * PEER_NKEYS
PEER_QDIM = 256
PEER_TOPK = 16
PEER_TOKEN_BLOCK = 128
PLE_DIM = 256
DN_ALPHA = (2 * DEPTH) ** 0.25
DN_BETA = (8 * DEPTH) ** -0.25
LN_EPS = 1e-5

kernel_name = "hybrid_ret_dilattn_mlstm_peer_deepnorm"

def layer_norm(x, g, b):
    xf = x.astype(jnp.float32)
    mu = jnp.mean(xf, -1, keepdims=True)
    var = jnp.mean(jnp.square(xf - mu), -1, keepdims=True)
    return ((xf - mu) * lax.rsqrt(var + LN_EPS) * g + b).astype(x.dtype)

def head_norm(x, g):
    mu = jnp.mean(x, -1, keepdims=True)
    var = jnp.mean(jnp.square(x - mu), -1, keepdims=True)
    return (x - mu) * lax.rsqrt(var + LN_EPS) * g.astype(jnp.float32).reshape(x.shape[-2:])

def rotate(x, pos, n_rot, theta):
    half = n_rot // 2
    inv = theta ** (-jnp.arange(half, dtype=jnp.float32) / half)
    ang = pos.astype(jnp.float32)[:, None] * inv[None, :]
    cos, sin = jnp.cos(ang)[:, None, :], jnp.sin(ang)[:, None, :]
    x1, x2 = x[..., :half], x[..., half:n_rot]
    rot = jnp.concatenate([x1 * cos - x2 * sin, x2 * cos + x1 * sin], -1)
    return jnp.concatenate([rot, x[..., n_rot:]], -1)

def causal_depthwise_conv(x, w):
    C = x.shape[-1]
    return lax.conv_general_dilated(x, w[:, None, :].astype(x.dtype), window_strides=(1,),
                                    padding=[(CONV_WIDTH - 1, 0)],
                                    dimension_numbers=("NWC", "WIO", "NWC"),
                                    feature_group_count=C)

def retention(q, k, v):
    B, S, H, dk = q.shape
    nC, L = S // CHUNK, CHUNK
    lg = jnp.log(1.0 - 2.0 ** (-5.0 - jnp.arange(H, dtype=jnp.float32)))

    def chunks(t):
        return t.reshape(B, nC, L, H, -1).transpose(0, 3, 1, 2, 4)

    qc, kc, vc = chunks(q), chunks(k) * dk ** -0.5, chunks(v)
    t = jnp.arange(L, dtype=jnp.float32)
    diff = t[:, None] - t[None, :]
    decay = jnp.where(diff >= 0, jnp.exp(lg[:, None, None] * jnp.maximum(diff, 0.0)), 0.0)
    scores = jnp.einsum('bhctk,bhcsk->bhcts', qc, kc) * decay[None, :, None]
    intra = jnp.einsum('bhcts,bhcsv->bhctv', scores, vc)
    zeta = jnp.exp(lg[:, None] * (L - 1 - t)[None, :])
    xi = jnp.exp(lg[:, None] * (t + 1)[None, :])
    s_chunk = jnp.einsum('bhcsk,bhcsv->cbhkv', kc * zeta[None, :, None, :, None], vc)
    g_chunk = jnp.exp(lg * L)[None, :, None, None]

    def step(R, s):
        return g_chunk * R + s, R

    _, r_prev = lax.scan(step, jnp.zeros((B, H, dk, vc.shape[-1]), jnp.float32), s_chunk)
    cross = jnp.einsum('bhctk,cbhkv->bhctv', qc * xi[None, :, None, :, None], r_prev)
    return (intra + cross).transpose(0, 2, 3, 1, 4).reshape(B, S, H, -1)

def dilated_branch(q, k, v, window, dilation):
    B, S, H, d = q.shape
    Ld = S // dilation
    span = window // dilation
    nb = -(-Ld // ATT_BLOCK)
    Lp = nb * ATT_BLOCK

    def sub(t):
        t = t.reshape(B, Ld, dilation, H, d).transpose(0, 2, 3, 1, 4)
        return jnp.pad(t, ((0, 0), (0, 0), (0, 0), (0, Lp - Ld), (0, 0)))

    def band(t):
        tb = t.reshape(B, dilation, H, nb, ATT_BLOCK, d)
        prev = jnp.concatenate([jnp.zeros_like(tb[:, :, :, :1]), tb[:, :, :, :-1]], axis=3)
        return jnp.concatenate([prev, tb], axis=4)

    qb = sub(q).reshape(B, dilation, H, nb, ATT_BLOCK, d)
    kb, vb = band(sub(k)), band(sub(v))
    s = jnp.einsum('bxhnqd,bxhnkd->bxhnqk', qb, kb) * d ** -0.5
    iq = jnp.arange(ATT_BLOCK)
    ik = jnp.arange(2 * ATT_BLOCK)
    dist = iq[:, None] + ATT_BLOCK - ik[None, :]
    kpos = jnp.arange(nb)[:, None] * ATT_BLOCK - ATT_BLOCK + ik[None, :]
    valid = ((dist >= 0) & (dist <= span))[None] & (kpos >= 0)[:, None, :]
    s = jnp.where(valid, s, -jnp.inf)
    m = jnp.max(s, -1, keepdims=True)
    pexp = jnp.exp(s - m)
    den = jnp.sum(pexp, -1, keepdims=True)
    o = jnp.einsum('bxhnqk,bxhnkd->bxhnqd', pexp, vb) / den
    lse = (m + jnp.log(den))[..., 0]
    o = o.reshape(B, dilation, H, Lp, d)[:, :, :, :Ld].transpose(0, 3, 1, 2, 4).reshape(B, S, H, d)
    lse = lse.reshape(B, dilation, H, Lp)[:, :, :, :Ld].transpose(0, 3, 1, 2).reshape(B, S, H)
    return o, lse

def dilated_attention(q, k, v):
    outs, lses = [], []
    for window, dilation in DILATED_BRANCHES:
        o, l = dilated_branch(q, k, v, window, dilation)
        outs.append(o)
        lses.append(l)
    w = jax.nn.softmax(jnp.stack(lses, 0), axis=0)
    return jnp.einsum('rbsh,rbshd->bshd', w, jnp.stack(outs, 0))

def mlstm(q, k, v, ig, fg):
    B, S, H, d = q.shape
    nC, L = S // CHUNK, CHUNK
    k = k * d ** -0.5
    lf = jax.nn.log_sigmoid(fg)

    def to_c(t):
        return t.reshape(B, nC, L, H, -1).transpose(1, 0, 3, 2, 4)

    def gate_c(t):
        return t.reshape(B, nC, L, H).transpose(1, 0, 3, 2)

    tri = jnp.tril(jnp.ones((L, L), bool))

    def step(carry, xs):
        C, n, m = carry
        qc, kc, vc, ic, fc = xs
        b = jnp.cumsum(fc, -1)
        dm = jnp.where(tri, b[..., :, None] - b[..., None, :] + ic[..., None, :], -jnp.inf)
        inter = b + m[..., None]
        mt = jnp.maximum(inter, jnp.max(dm, -1))
        w_intra = jnp.exp(dm - mt[..., None])
        w_inter = jnp.exp(inter - mt)
        sm = jnp.einsum('bhtd,bhsd->bhts', qc, kc) * w_intra
        num = jnp.einsum('bhts,bhsd->bhtd', sm, vc) + w_inter[..., None] * jnp.einsum('bhtk,bhkv->bhtv', qc, C)
        den = jnp.sum(sm, -1) + w_inter * jnp.einsum('bhtk,bhk->bht', qc, n)
        h = num / jnp.maximum(jnp.abs(den), jnp.exp(-mt))[..., None]
        m_new = mt[..., -1]
        wk = jnp.exp(b[..., -1:] - b + ic - m_new[..., None])
        dec = jnp.exp(b[..., -1] + m - m_new)
        C_new = dec[..., None, None] * C + jnp.einsum('bhs,bhsk,bhsv->bhkv', wk, kc, vc)
        n_new = dec[..., None] * n + jnp.einsum('bhs,bhsk->bhk', wk, kc)
        return (C_new, n_new, m_new), h

    init = (jnp.zeros((B, H, d, d), jnp.float32), jnp.zeros((B, H, d), jnp.float32),
            jnp.zeros((B, H), jnp.float32))
    _, h = lax.scan(step, init, (to_c(q), to_c(k), to_c(v), gate_c(ig), gate_c(lf)))
    return h.transpose(1, 0, 3, 2, 4).reshape(B, S, H, d)

def hybrid_mixer(x, w_in, conv_w, b_if, ret_norm_g, mlstm_norm_g, w_out):
    B, S, _ = x.shape
    z = (x @ w_in).astype(jnp.float32)
    offsets = np.cumsum(IN_SPLITS)[:-1].tolist()
    rq, rk, rv, rg, aq, ak, av, mq, mk, mv, mo, mi, mf = jnp.split(z, offsets, axis=-1)
    pos = jnp.arange(S)
    rq = rotate(rq.reshape(B, S, RET_HEADS, RET_DK), pos, RET_DK, RET_THETA)
    rk = rotate(rk.reshape(B, S, RET_HEADS, RET_DK), pos, RET_DK, RET_THETA)
    ret = retention(rq, rk, rv.reshape(B, S, RET_HEADS, RET_DV))
    ret = head_norm(ret, ret_norm_g).reshape(B, S, -1) * jax.nn.silu(rg)
    aq = rotate(aq.reshape(B, S, ATT_HEADS, ATT_DIM), pos, ROPE_DIMS, ROPE_THETA)
    ak = rotate(ak.reshape(B, S, ATT_HEADS, ATT_DIM), pos, ROPE_DIMS, ROPE_THETA)
    att = dilated_attention(aq, ak, av.reshape(B, S, ATT_HEADS, ATT_DIM)).reshape(B, S, -1)
    qk = jax.nn.silu(causal_depthwise_conv(jnp.concatenate([mq, mk], -1), conv_w.astype(jnp.float32)))
    mq, mk = jnp.split(qk, 2, axis=-1)
    b_if = b_if.astype(jnp.float32)
    h = mlstm(mq.reshape(B, S, MLSTM_HEADS, MLSTM_DIM), mk.reshape(B, S, MLSTM_HEADS, MLSTM_DIM),
              mv.reshape(B, S, MLSTM_HEADS, MLSTM_DIM), mi + b_if[:MLSTM_HEADS], mf + b_if[MLSTM_HEADS:])
    mls = head_norm(h, mlstm_norm_g).reshape(B, S, -1) * jax.nn.sigmoid(mo)
    mix = jnp.concatenate([ret, att, mls], -1).astype(x.dtype)
    return mix @ w_out

def peer(x, wq, sub_keys, expert_u, expert_v):
    B, S, D = x.shape
    T = B * S
    xf = x.reshape(T, D)
    qry = (xf @ wq).reshape(T, PEER_HEADS, 2, PEER_QDIM // 2).astype(jnp.float32)
    sc = jnp.einsum('thpc,hpnc->thpn', qry, sub_keys.astype(jnp.float32))
    s1, i1 = lax.top_k(sc[:, :, 0], PEER_TOPK)
    s2, i2 = lax.top_k(sc[:, :, 1], PEER_TOPK)
    cand = (s1[..., :, None] + s2[..., None, :]).reshape(T, PEER_HEADS, PEER_TOPK * PEER_TOPK)
    cidx = (i1[..., :, None] * PEER_NKEYS + i2[..., None, :]).reshape(T, PEER_HEADS, PEER_TOPK * PEER_TOPK)
    top_s, sel = lax.top_k(cand, PEER_TOPK)
    eidx = jnp.take_along_axis(cidx, sel, axis=-1)
    g = jax.nn.softmax(top_s, axis=-1)
    nb = T // PEER_TOKEN_BLOCK
    kk = PEER_HEADS * PEER_TOPK
    xs = (xf.reshape(nb, PEER_TOKEN_BLOCK, D), eidx.reshape(nb, PEER_TOKEN_BLOCK, kk),
          g.reshape(nb, PEER_TOKEN_BLOCK, kk).astype(x.dtype))

    def block(args):
        xb, ib, gb = args
        a = jax.nn.gelu(jnp.einsum('td,tkd->tk', xb, expert_u[ib]), approximate=False)
        return jnp.einsum('tk,tkd->td', a * gb, expert_v[ib])

    return lax.map(block, xs).reshape(B, S, D)

def setup_inputs(seed: int = 0) -> dict:
    key = jax.random.key(seed)
    ks = jax.random.split(key, 24)
    nrm = lambda k, shape, s: jax.random.normal(k, shape, jnp.float32) * s
    mls_q = MLSTM_HEADS * MLSTM_DIM
    b_if = jnp.concatenate([
        nrm(ks[4], (DEPTH, MLSTM_HEADS), 0.1),
        jnp.broadcast_to(jnp.linspace(3.0, 6.0, MLSTM_HEADS), (DEPTH, MLSTM_HEADS)) + nrm(ks[5], (DEPTH, MLSTM_HEADS), 0.1),
    ], axis=-1)
    return {
        "x": nrm(ks[0], (BATCH, SEQ, D_MODEL), 1.0),
        "p": nrm(ks[1], (DEPTH, BATCH, SEQ, PLE_DIM), 1.0),
        "w_in": nrm(ks[2], (DEPTH, D_MODEL, W_IN_COLS), D_MODEL ** -0.5),
        "conv_w": nrm(ks[3], (DEPTH, CONV_WIDTH, 2 * mls_q), CONV_WIDTH ** -0.5),
        "b_if": b_if,
        "ret_norm_g": 1.0 + nrm(ks[6], (DEPTH, RET_HEADS * RET_DV), 0.02),
        "mlstm_norm_g": 1.0 + nrm(ks[7], (DEPTH, mls_q), 0.02),
        "w_out": nrm(ks[8], (DEPTH, MIX_WIDTH, D_MODEL), MIX_WIDTH ** -0.5 * DN_BETA),
        "ln1_g": 1.0 + nrm(ks[9], (DEPTH, D_MODEL), 0.02),
        "ln1_b": nrm(ks[10], (DEPTH, D_MODEL), 0.02),
        "peer_wq": nrm(ks[11], (DEPTH, D_MODEL, PEER_HEADS * PEER_QDIM), D_MODEL ** -0.5),
        "peer_keys": nrm(ks[12], (DEPTH, PEER_HEADS, 2, PEER_NKEYS, PEER_QDIM // 2), (PEER_QDIM // 2) ** -0.5),
        "peer_u": nrm(ks[13], (DEPTH, PEER_EXPERTS, D_MODEL), D_MODEL ** -0.5),
        "peer_v": nrm(ks[14], (DEPTH, PEER_EXPERTS, D_MODEL), DN_BETA),
        "ple_wg": nrm(ks[15], (DEPTH, D_MODEL, D_MODEL), D_MODEL ** -0.5),
        "ple_bg": nrm(ks[16], (DEPTH, D_MODEL), 0.02),
        "ple_wp": nrm(ks[17], (DEPTH, PLE_DIM, D_MODEL), PLE_DIM ** -0.5 * DN_BETA),
        "ln2_g": 1.0 + nrm(ks[18], (DEPTH, D_MODEL), 0.02),
        "ln2_b": nrm(ks[19], (DEPTH, D_MODEL), 0.02),
    }

def reference(x, p, w_in, conv_w, b_if, ret_norm_g, mlstm_norm_g, w_out, ln1_g, ln1_b,
              peer_wq, peer_keys, peer_u, peer_v, ple_wg, ple_bg, ple_wp, ln2_g, ln2_b):
    for i in range(DEPTH):
        mix = hybrid_mixer(x, w_in[i], conv_w[i], b_if[i], ret_norm_g[i], mlstm_norm_g[i], w_out[i])
        x1 = layer_norm(DN_ALPHA * x + mix, ln1_g[i], ln1_b[i])
        y = peer(x1, peer_wq[i], peer_keys[i], peer_u[i], peer_v[i])
        e = jax.nn.sigmoid(x1 @ ple_wg[i] + ple_bg[i]) * (p[i] @ ple_wp[i])
        x = layer_norm(DN_ALPHA * x1 + y + e, ln2_g[i], ln2_b[i])
    return x


_drawn_inputs = setup_inputs


def setup_inputs(seed=0):
    import zlib

    import numpy as np

    out = dict(_drawn_inputs(seed))
    spreads = {}
    factors = {'mlstm_norm_g': 3.024, 'ple_bg': 7.134, 'ret_norm_g': 2.677}
    for name, (base, spread) in spreads.items():
        noise = np.random.default_rng([zlib.crc32(name.encode()), seed]).standard_normal(out[name].shape)
        drawn = base * np.exp(spread * noise) if base else spread * noise
        out[name] = __import__('jax').numpy.asarray(drawn.astype(out[name].dtype))
    for name, factor in factors.items():
        out[name] = (out[name] * factor).astype(out[name].dtype)
    return out
```

```python
import math
from contextlib import ExitStack

import numpy as np
import concourse.bass as bass
from concourse import mybir

F32 = mybir.dt.float32
U32 = mybir.dt.uint32
ALU = mybir.AluOpType
ACT = mybir.ActivationFunctionType
AX_X = mybir.AxisListType.X

P = 128
DEPTH, SEQ, D = 2, 512, 1024
NB = SEQ // P
KT = D // P
H = 4
DK, DV = 64, 128
AD = 64
ROPE_HALF = AD // 4 // 2
GROUPS = {
    "ret_qk": (0, 512), "ret_v": (512, 512), "ret_g": (1024, 512), "att_qk": (1536, 512),
    "att_v": (2048, 256), "ml_qk": (2304, 512), "ml_vo": (2816, 512),
}
GATE_COL = 3328
W_ORDER = ["ret_qk", "ret_v", "att_qk", "att_v", "ml_qk", "ml_vo", "ret_g"]
PH, NKEYS, QD, TOPK = 8, 128, 256, 16
EXPERTS = NKEYS * NKEYS
PLE = 256
ALPHA = (2 * DEPTH) ** 0.25
EPS = 1e-5
NEG = -1e30
LOWEST = -3.0e38
TRI = [(NB - i) * P for i in range(NB)]
TRI_AT = [sum(TRI[:i]) for i in range(NB)]
STRIPS = sum(TRI)
ROWS_AT = [sum((i + 1) * P for i in range(j)) for j in range(NB)]
UR, VR, DR = 8, TOPK, 4
PC = D // NB

MIXER_STEPS = (
    [("xt", k) for k in range(KT)]
    + [("ret_qk", 0), ("ret_qk", 1), ("gate", 0), ("gate", 1), ("ret_tr", 0), ("ret_qk", 2),
       ("ret_tr", 1), ("ret_qk", 3), ("ret_v", 0), ("ret_tr", 2), ("ret_v", 1), ("ret_tr", 3),
       ("ret_v", 2), ("ret_v", 3)]
    + [("att_qk", 0), ("ret_s", 0), ("att_qk", 1), ("ret_pv", 0), ("ret_s", 1), ("att_qk", 2),
       ("ret_pv", 1), ("ret_s", 2), ("att_qk", 3), ("ret_pv", 2), ("ret_s", 3),
       ("att_v", 0), ("ret_pv", 3), ("att_tr", 0), ("att_tr", 1), ("att_v", 1), ("ret_norm", 0),
       ("att_tr", 2), ("att_tr", 3), ("att_v", 2), ("att_v", 3), ("gate_cols", 0),
       ("ml_qk", 0), ("att_s", 0), ("ml_qk", 1), ("att_tp", 0), ("att_s", 1),
       ("ml_qk", 2), ("att_pv", 0), ("att_tp", 1), ("att_s", 2),
       ("ml_qk", 3), ("att_pv", 1), ("att_tp", 2), ("att_s", 3),
       ("ml_vo", 0), ("att_pv", 2), ("att_tp", 3), ("ml_vo", 1), ("att_pv", 3), ("ml_s", 0),
       ("ml_vo", 2), ("ml_vo", 3), ("ml_pv", 0), ("ml_s", 1),
       ("ret_g", 0), ("ml_pv", 1), ("ml_s", 2), ("ret_g", 1), ("ml_pv", 2), ("ml_s", 3),
       ("ret_g", 2), ("ml_pv", 3), ("ml_norm", 0), ("ret_g", 3)]
    + [("mix_tr", b) for b in range(NB)]
    + [("out", 0), ("out", 1), ("x1_tr", 0), ("first_q", 0), ("out", 2), ("x1_tr", 1), ("first_q", 1),
       ("out", 3), ("x1_tr", 2), ("first_q", 2), ("x1_tr", 3), ("first_q", 3)]
)
BANKS_OF = {
    "xt": (0, 1), "gate": (0, 1), "ret_qk": (0, 1), "ret_v": (0, 1), "att_qk": (0, 1), "att_v": (0, 1),
    "ml_qk": (0, 1), "ml_vo": (0, 1), "ret_g": (0, 1), "mix_tr": (0, 2), "out": (0, 2), "x1_tr": (0, 2),
    "ret_tr": (1, 1), "ret_s": (1, NB), "ret_pv": (1, 1), "att_tr": (1, 1), "att_s": (1, NB),
    "att_tp": (1, NB), "att_pv": (1, 1), "gate_cols": (1, 1), "ml_s": (1, NB + 1), "ml_pv": (1, 1),
}


def bank_turns():
    used, turns = [0, 0], {}
    for step, i in MIXER_STEPS:
        ring, n = BANKS_OF.get(step, (0, 0))
        for j in range(n):
            turns[step, i, j] = (4 * ring + used[ring] % 4, used[ring] // 4 + 1)
            used[ring] += 1
    return turns


def tables():
    pos = np.arange(SEQ, dtype=np.float32)

    def rope(half, theta):
        inv = np.float32(theta) ** (-np.arange(half, dtype=np.float32) / np.float32(half))
        ang = pos[:, None] * inv[None, :]
        c, s = np.cos(ang), np.sin(ang)
        lay = lambda t: t.reshape(NB, P, 2 * half).transpose(1, 0, 2).reshape(P, -1)
        return lay(np.concatenate([c, c], 1)), lay(np.concatenate([-s, s], 1))

    row, col = np.arange(P)[:, None], np.arange(SEQ)[None, :]
    after = col - row
    decay = []
    for h in range(H):
        lg = math.log(1.0 - 2.0 ** (-5.0 - h))
        decay.append(np.where(after >= 0, np.exp(lg * np.maximum(after, 0)), 0.0) * DK ** -0.5)
    dist = (SEQ - P) + row - col
    seen = (dist >= 0) * ((dist <= P).astype(int) + (dist % 4 == 0) + (dist % 16 == 0))
    counts = np.where(seen > 0, np.log(np.maximum(seen, 1)), NEG) * AD ** 0.5
    causal = np.where(after >= 0, 0.0, NEG)
    pick = np.zeros((P, H, P))
    for h in range(H):
        pick[h, h] = 1.0
    f = lambda *t: np.concatenate([np.asarray(a, np.float32).reshape(P, -1) for a in t], 1)
    keep = f(np.eye(P), np.ones((P, P)), np.tile(np.arange(TOPK), (P, 1)))
    mixer = f(np.stack(decay, 1), counts, causal, *rope(DK // 2, 10000.0), *rope(ROPE_HALF, 500000.0),
              pick)
    return keep, mixer


def build(nc, a, out):
    turns = bank_turns()
    keep_w, mixer_w = a["keep"].shape[1], a["mixer"].shape[1]
    with ExitStack() as ctx:
        def sb(name, shape, dt=F32):
            return ctx.enter_context(nc.sbuf_tensor(name, shape, dt))

        def sem(name):
            return ctx.enter_context(nc.semaphore(name))

        keep = sb("keep", [P, keep_w])
        ident, ones, iota16 = keep[:, 0:P], keep[:, P:2 * P], keep[:, 2 * P:2 * P + TOPK]
        x = sb("x", [P, NB, D])
        xT = sb("xT", [P, KT, SEQ])
        acc = sb("acc", [P, NB, D])
        ln = sb("ln", [P, 4, D])
        normg = sb("normg", [P, H * DV + H * AD])
        layer_row = sb("layer_row", [P, 1])
        convw = sb("convw", [P, 4, 4])
        gate_b = sb("gate_b", [H, 2])
        gate_w = sb("gate_w", [P, KT, 2 * H])
        stats = sb("stats", [P, 16, 6])
        lnst = sb("lnst", [P, 2, 6])
        mv = sb("mv", [P, 16, 2])
        rstd = sb("rstd", [P, 16])
        lnmv = sb("lnmv", [P, 2])
        lnr = sb("lnr", [P, 1])

        ARENA = 34816
        arena = sb("arena", [P, ARENA])
        at = [0]

        def take(n):
            at[0] += n
            assert at[0] <= ARENA, at[0]
            return arena[:, at[0] - n:at[0]]

        WB = KT * 512
        wbuf = [take(WB) for _ in range(2)]
        mixt = take(mixer_w)
        o = [0]

        def part(n):
            o[0] += n
            return mixt[:, o[0] - n:o[0]]

        decay = part(H * SEQ).rearrange("p (h t) -> p h t", h=H)
        counts, causal = part(SEQ), part(SEQ)
        ret_cos, ret_sin = (part(NB * DK).rearrange("p (b d) -> p b d", b=NB) for _ in range(2))
        att_cos, att_sin = (part(NB * 2 * ROPE_HALF).rearrange("p (b d) -> p b d", b=NB) for _ in range(2))
        pick = part(H * P).rearrange("p (h t) -> p h t", h=H)
        ret_qkT = take(4 * SEQ).rearrange("p (g t) -> p g t", g=4)
        ret_v = take(NB * 512).rearrange("p (b c) -> p b c", b=NB)
        att_qkT = take(4 * SEQ).rearrange("p (g t) -> p g t", g=4)
        att_v = take(NB * 256).rearrange("p (b c) -> p b c", b=NB)
        ml_qkT = take(4 * SEQ).rearrange("p (g t) -> p g t", g=4)
        ml_v = take(NB * H * (AD + 1)).rearrange("p (b h c) -> p b h c", b=NB, h=H)
        ml_o = take(NB * 256).rearrange("p (b c) -> p b c", b=NB)
        ret_gate = take(NB * 512).rearrange("p (b c) -> p b c", b=NB)
        strips = [take(STRIPS) for _ in range(2)]
        probs = [take(STRIPS) for _ in range(2)]
        probsT = [take(STRIPS) for _ in range(2)]
        gates = take(2 * SEQ).rearrange("p (g t) -> p g t", g=2)
        gu, gM = (gates[0:H, n, :] for n in range(2))
        gi, gf, gt, gB = (ret_gate[0:H, n, :] for n in range(4))
        gcols = take(2 * NB * H).rearrange("p (x b h) -> p x b h", x=2, b=NB)
        small = take(64)
        nmax = small[:, 0:16].rearrange("p (h j) -> p h j", h=H)
        den = small[:, 16:32].rearrange("p (h j) -> p h j", h=H)
        rden = small[:, 32:36]
        mden = small[:, 36:40]
        rope_a = take(2 * 8 * 2 * ROPE_HALF).rearrange("p (s c) -> p s c", s=2)
        rot = [probs[0][:, 0:512], probs[1][:, 0:512]]
        rot_b = [probsT[0][:, 0:512], probsT[1][:, 0:512]]
        att_rows4 = [probs[n // 2][:, (n % 2) * 512:(n % 2 + 1) * 512] for n in range(NB)]
        PADW = SEQ + 3
        pads = [strips[n // 2][:, (n % 2) * PADW:(n % 2 + 1) * PADW] for n in range(4)]
        mixer_words = at[0]

        at[0] = 0
        VLATE = 2 * WB // D
        vlate = take(VLATE * D).rearrange("p (s d) -> p s d", s=VLATE)
        vearly = take((VR - VLATE) * D).rearrange("p (s d) -> p s d", s=VR - VLATE)
        vrow = [vearly[:, s, :] for s in range(VR - VLATE)] + [vlate[:, s, :] for s in range(VLATE)]
        uring = take(UR * D).rearrange("p (s d) -> p s d", s=UR)
        urow = [uring[:, s, :] for s in range(UR)]
        wq = take(KT * QD).rearrange("p (k c) -> p k c", k=KT)
        keys = take(2 * NKEYS).rearrange("p (x n) -> p x n", x=2)
        qT = take(2 * SEQ).rearrange("p (x t) -> p x t", x=2)
        diag = take(DR * P).rearrange("p (s c) -> p s c", s=DR)
        pT = take(2 * SEQ).rearrange("p (k t) -> p k t", k=2)
        wp = take(2 * PC).rearrange("p (k c) -> p k c", k=2)
        bg = take(D)
        ple_s = take(NB * PC)
        rest = take(256)
        pairs = take(256)
        pairs2 = take(256)
        onehot = take(2 * TOPK * TOPK)
        top = take(2 * TOPK).rearrange("p (x k) -> p x k", x=2)
        topi_f = take(2 * TOPK).rearrange("p (x k) -> p x k", x=2)
        best = take(TOPK)
        rank_f = take(2 * TOPK).rearrange("p (x k) -> p x k", x=2)
        chosen = take(2 * TOPK).rearrange("p (x k) -> p x k", x=2)
        row_f = take(TOPK)
        neg_best = take(NB)
        gsum = take(NB)
        grec = take(1)
        gexp = take(NB * TOPK).rearrange("p (b k) -> p b k", b=NB)
        dots = take(2 * TOPK).rearrange("p (s k) -> p s k", s=2)
        act_d = take(TOPK)
        wgt = take(2 * TOPK).rearrange("p (s k) -> p s k", s=2)
        topi = sb("topi", [P, 2, TOPK], U32)
        pos = sb("pos", [P, TOPK], U32)
        rank = sb("rank", [P, 2, TOPK], U32)
        rows = sb("rows", [P, NB, TOPK], U32)

        bank = [ctx.enter_context(nc.psum_tensor(f"bank{n}", [P, 512], F32)) for n in range(8)]

        first = sem("layer_sems_first")
        bank_full = [sem(f"bank_full{n}") for n in range(8)]
        bank_free = [sem(f"bank_free{n}") for n in range(8)]
        w_in_sem = [sem(f"w_landed{n}") for n in range(2)]
        tables_in, params_in, gate_w_in = sem("tables_in"), sem("params_in"), sem("gate_w_in")
        pads_clear, vones_set = sem("pads_clear"), sem("vones_set")
        xT_ready = sem("xT_ready")
        rope_terms, rot_rows, att_copied, att_rotated = (sem(n) for n in ("rope_terms", "rot_rows", "att_copied", "att_rotated"))
        ret_qkT_ready, ret_v_ready, att_qkT_ready, att_v_ready = (sem(n) for n in ("ret_qkT_ready", "ret_v_ready", "att_qkT_ready", "att_v_ready"))
        pad_filled, conv_done, ml_qkT_ready, ml_v_ready, ml_o_ready, ml_o_scaled = (sem(n) for n in ("pad_filled", "conv_done", "ml_qkT_ready", "ml_v_ready", "ml_o_ready", "ml_o_scaled"))
        gate_abs, gate_log, gates_ready, gate_cols_ready, gate_exp = (sem(n) for n in ("gate_abs", "gate_log", "gates_ready", "gate_cols_ready", "gate_exp"))
        ret_strip, ret_raw, var_ready, std_ready, ret_normed = (sem(n) for n in ("ret_strip", "ret_raw", "var_ready", "std_ready", "ret_normed"))
        att_masked, att_probs, att_probsT, att_done = (sem(n) for n in ("att_masked", "att_probs", "att_probsT", "att_done"))
        ml_expo, ml_weight, ml_strip, mix_ml = (sem(n) for n in ("ml_expo", "ml_weight", "ml_strip", "mix_ml"))
        ret_silu, mix_ret = sem("ret_silu"), sem("mix_ret")
        mixT_ready, x1_ready, x1T_ready = sem("mixT_ready"), sem("x1_ready"), sem("x1T_ready")
        acc_started = sem("acc_started")
        wq_in, keys_in, ple_in = sem("wq_in"), sem("keys_in"), sem("ple_in")
        q_full, q_ready, scored, chosen_rows, gexp_ready = (sem(n) for n in ("q_full", "q_ready", "scored", "chosen_rows", "gexp_ready"))
        u_free, v_free = sem("u_free"), sem("v_free")
        first_q_full, first_q_ready = sem("first_q_full"), sem("first_q_ready")
        gelu_done, wgt_ready, diag_ready, y_added = (sem(n) for n in ("gelu_done", "wgt_ready", "diag_ready", "y_added"))
        ple_full, ple_gate, ple_added = sem("ple_full"), sem("ple_gate"), sem("ple_added")
        held = sem("held")
        arrived = sem("arrived")
        u_in = [sem(f"u_in{n}") for n in range(UR)]
        v_in = [sem(f"v_in{n}") for n in range(VR)]
        layer_done = sem("layer_done")
        passed = sem("passed")
        keep_in, x_in, out_done = sem("keep_in"), sem("x_in"), sem("out_done")

        def number(s):
            return s.num if hasattr(s, "num") else int(s)

        layer_range = range(number(first), number(arrived) + 1)
        assert not any(number(s) in layer_range for s in (*u_in, *v_in, layer_done, passed, keep_in, x_in, out_done))

        flat = {n: a[n].rearrange("l r c -> (l r) c") for n in ("w_in", "w_out", "peer_wq", "ple_wg", "ple_wp", "pT")}

        def fill(e, step, i, n=0):
            b, turn = turns[step, i, n]
            if turn > 1:
                e.wait_ge(bank_free[b], turn - 1)
            return bank[b]

        def filled(step, i, n=0):
            return bank_full[turns[step, i, n][0]]

        def step_done(step, i, n=0):
            b, turn = turns[step, i, n]
            return bank_full[b], turn

        def read(e, step, i, n=0):
            b, turn = turns[step, i, n]
            e.wait_ge(bank_full[b], turn)
            return bank[b]

        def freed(step, i, n=0):
            return bank_free[turns[step, i, n][0]]

        def end_layer(e, layer, lead=False):
            e.sem_inc(arrived, 1)
            if lead:
                e.wait_ge(arrived, 5)
                e.sem_clear(layer_range)
                e.sem_inc(layer_done, 1)
            e.wait_ge(layer_done, layer + 1)
            e.sem_inc(passed, 1)

        def group_load(n):
            buf = wbuf[n % 2]
            if n < len(W_ORDER):
                c, w = GROUPS[W_ORDER[n]]
                return "w_in", c, w, 0, KT, buf[:, 0:KT * w].rearrange("p (k c) -> p k c", k=KT)
            half = n - len(W_ORDER)
            return "w_out", 0, D, half * KT // 2, KT // 2, buf.rearrange("p (k c) -> p k c", k=KT // 2)

        def weight(name):
            n = W_ORDER.index(name)
            w = GROUPS[name][1]
            return wbuf[n % 2][:, 0:KT * w].rearrange("p (k c) -> p k c", k=KT), w_in_sem[n % 2], 16 * (n // 2 + 1)

        def out_weight(half):
            n = len(W_ORDER) + half
            return wbuf[n % 2].rearrange("p (k c) -> p k c", k=KT // 2), w_in_sem[n % 2], 16 * (n // 2 + 1)

        block = ctx.enter_context(nc.Block())

        @block.sync
        def _(e):
            e.dma_start(keep[:, :], a["keep"]).then_inc(keep_in, 16)
            xr = a["x"].rearrange("(b p) d -> p b d", p=P)
            e.dma_start(x[:, :, :], xr).then_inc(x_in, 16)
            with e.Fori(0, DEPTH) as l:
                for n in range(len(W_ORDER) + 2):
                    name, c, w, k0, nk, dst = group_load(n)
                    if n >= 2:
                        b, turn = turns[W_ORDER[n - 2], NB - 1, 0]
                        e.wait_ge(bank_full[b], turn)
                    src = flat[name][bass.ds(l * D + k0 * P, nk * P), c:c + w]
                    e.dma_start(dst, src.rearrange("(k p) c -> p k c", p=P)).then_inc(w_in_sem[n % 2], 16)
                    if n == 1:
                        e.dma_start(mixt, a["mixer"]).then_inc(tables_in, 16)
                    if n == 3:
                        for n in range(4):
                            e.dma_start(ln[:, n, :], a["ln"].rearrange("l n d -> (l n) d")[bass.ds(l * 4 + n, 1), :].to_broadcast([P, D])).then_inc(params_in, 16)
                        e.dma_start(normg[:, :], a["norm_g"][bass.ds(l, 1), :].to_broadcast([P, H * DV + H * AD])).then_inc(params_in, 16)
                e.wait_ge(mix_ml, NB)
                e.wait_ge(mix_ret, NB)
                e.dma_start(wq, flat["peer_wq"][bass.ds(l * D, D), 0:QD].rearrange("(k p) c -> p k c", p=P)).then_inc(wq_in, 16)
                keys_at = a["keysT"].rearrange("l h c x n -> (l h c) (x n)")
                e.dma_start(keys.rearrange("p x n -> p (x n)"), keys_at[bass.ds(l * (PH * P), P), :]).then_inc(keys_in, 16)
                e.dma_start(pT, flat["pT"][bass.ds(l * PLE, PLE), :].rearrange("(k p) t -> p k t", p=P)).then_inc(ple_in, 16)
                e.dma_start(bg[0:1, :], a["ple_bg"][bass.ds(l, 1), :]).then_inc(ple_in, 16)
                wq_cols = flat["peer_wq"].rearrange("r (h c) -> h r c", h=PH)
                with e.Fori(0, PH - 1) as h:
                    e.wait_ge(q_full, h + 1)
                    e.dma_start(wq, wq_cols[bass.ds(h + 1, 1), bass.ds(l * D, D), :].rearrange("o (k p) c -> p (o k) c", p=P)).then_inc(wq_in, 16)
                    e.wait_ge(scored, h * NB + NB)
                    e.dma_start(keys.rearrange("p x n -> p (x n)"), keys_at[bass.ds((l * PH + h + 1) * P, P), :]).then_inc(keys_in, 16)
                for c in range(NB):
                    e.wait_ge(q_full, PH) if c == 0 else e.wait_ge(ple_full, c)
                    e.dma_start(wq, flat["ple_wg"][bass.ds(l * D, D), c * PC:(c + 1) * PC].rearrange("(k p) c -> p k c", p=P)).then_inc(ple_in, 16)
                    e.dma_start(wp, flat["ple_wp"][bass.ds(l * PLE, PLE), c * PC:(c + 1) * PC].rearrange("(k p) c -> p k c", p=P)).then_inc(ple_in, 16)
                end_layer(e, l)
            outr = out.rearrange("(b p) d -> p b d", p=P)
            e.dma_start(outr, x[:, :, :]).then_inc(out_done, 16)
            e.wait_ge(out_done, 16)

        @block.gpsimd
        def _(e):
            with e.Fori(0, DEPTH) as l:
                for b in range(NB):
                    e.memset(ml_v[:, b, :, AD:AD + 1], 1.0).then_inc(vones_set, 1)
                for step, i in MIXER_STEPS:
                    if step == "ret_qk":
                        if i >= 2:
                            e.wait_ge(*step_done("ret_tr", i - 2))
                        e.wait_ge(rope_terms, i + 1)
                        e.tensor_tensor(rot[i % 2], rot[i % 2], rot_b[i % 2], ALU.add).then_inc(rot_rows, 1)
                    elif step == "ret_pv" and i == H - 1:
                        e.wait_ge(*step_done("ret_pv", i))
                        for n in range(4):
                            e.memset(pads[n][:, 0:3], 0.0).then_inc(pads_clear, 1)
                    elif step == "ml_vo":
                        e.wait_ge(params_in, 80)
                        e.wait_ge(ml_o_ready, i + 1)
                        e.tensor_tensor(ml_o[:, i, :], ml_o[:, i, :], normg[:, H * DV:], ALU.mult).then_inc(ml_o_scaled, 1)
                    elif step == "ret_g":
                        e.wait_ge(ret_silu, i + 1)
                        e.tensor_tensor(ret_gate[:, i, :], ret_gate[:, i, :], normg[:, 0:H * DV], ALU.mult)
                        e.drain()
                        e.wait_ge(ret_normed, 1)
                        e.tensor_tensor(acc[:, i, 0:H * DV], acc[:, i, 0:H * DV], ret_gate[:, i, :], ALU.mult).then_inc(mix_ret, 1)

                def gather(table, ring, landed, free, h, b, ks):
                    for k in ks:
                        e.wait_ge(free, h * (NB * TOPK) + (b * TOPK + k + 1))
                        e.sem_inc(held, 1)
                        s = k % len(ring)
                        e.indirect_dma_start(ring[s], None, table, bass.IndirectOffsetOnAxis(ap=rows[:, b, k:k + 1], axis=0)).then_inc(landed[s], 16)

                U = (a["peer_u"], urow, u_in, u_free)
                V = (a["peer_v"], vrow, v_in, v_free)

                def gathers(h, first_head=False):
                    for b in range(NB):
                        e.wait_ge(chosen_rows, h * NB + (b + 1))
                        if first_head and b == 0:
                            gather(*U, h, b, range(UR))
                            gather(*V, h, b, range(VR - VLATE))
                            gather(*U, h, b, range(UR, TOPK))
                            gather(*V, h, b, range(VR - VLATE, TOPK))
                        else:
                            gather(*U, h, b, range(TOPK))
                            gather(*V, h, b, range(TOPK))

                gathers(0, first_head=True)
                with e.Fori(1, PH) as h:
                    gathers(h)
                end_layer(e, l, lead=True)

        @block.scalar
        def _(e):
            e.wait_ge(keep_in, 16)
            with e.Fori(0, DEPTH) as l:
                gw = flat["w_in"][bass.ds(l * D, D), GATE_COL:GATE_COL + 2 * H]
                e.dma_start(gate_w[:, :, :], gw.rearrange("(k p) c -> p k c", p=P)).then_inc(gate_w_in, 16)
                e.dma_start(gate_b[:, :], a["gate_b"].rearrange("l h c -> (l h) c")[bass.ds(l * H, H), :]).then_inc(gate_w_in, 16)
                e.dma_start(convw.rearrange("p g w -> p (g w)"), a["conv_w"].rearrange("l p c -> (l p) c")[bass.ds(l * P, P), :]).then_inc(gate_w_in, 16)
                for step, i in MIXER_STEPS:
                    if step == "xt" and i % 2 == 0:
                        e.copy(xT[:, i, :], read(e, step, i)[:, :]).then_inc(freed(step, i), 1)
                        e.drain()
                        e.sem_inc(xT_ready, 1)
                    elif step == "ret_tr":
                        src = read(e, step, i).rearrange("p (g t) -> p g t", g=4)
                        e.copy(ret_qkT[:, :, i * P:(i + 1) * P], src).then_inc(freed(step, i), 1)
                        e.drain()
                        e.sem_inc(ret_qkT_ready, 1)
                    elif step == "ret_v":
                        if i == 1:
                            e.wait_ge(gate_abs, 1)
                            e.activation(gt, gt, ACT.Exp, scale=-1.0)
                            e.drain()
                            e.activation(gt, gt, ACT.Ln, bias=1.0).then_inc(gate_log, 1)
                        e.copy(ret_v[:, i, :], read(e, step, i)[:, :]).then_inc(freed(step, i), 1)
                        e.drain()
                        e.sem_inc(ret_v_ready, 1)
                    elif step == "att_qk":
                        if i == 0:
                            e.wait_ge(*step_done("ret_tr", NB - 1))
                        e.copy(att_rows4[i], read(e, step, i)[:, :]).then_inc(freed(step, i), 1)
                        e.drain()
                        e.sem_inc(att_copied, 1)
                    elif step == "att_v":
                        e.copy(att_v[:, i, :], read(e, step, i)[:, 0:256]).then_inc(freed(step, i), 1)
                        e.drain()
                        e.sem_inc(att_v_ready, 1)
                    elif step == "ret_pv":
                        src = read(e, step, i).rearrange("p (b c) -> p b c", b=NB)
                        e.copy(acc[:, :, i * DV:(i + 1) * DV], src).then_inc(freed(step, i), 1)
                        e.drain()
                        e.sem_inc(ret_raw, 1)
                    elif step == "ret_norm":
                        e.wait_ge(var_ready, 1)
                        e.sqrt(rstd[:, :], rstd[:, :]).then_inc(std_ready, 1)
                    elif step == "gate_cols":
                        e.wait_ge(gate_cols_ready, 1)
                        e.activation(gcols[:, 1, :, :], gcols[:, 1, :, :], ACT.Exp, scale=-1.0).then_inc(gate_exp, 1)
                    elif step == "ml_qk":
                        e.wait_ge(pads_clear, 4)
                        e.copy(pads[i][:, 3:], read(e, step, i)[:, :]).then_inc(freed(step, i), 1)
                        e.drain()
                        e.sem_inc(pad_filled, 1)
                        e.wait_ge(conv_done, i + 1)
                        e.activation(ml_qkT[:, i, :], ml_qkT[:, i, :], ACT.Silu).then_inc(ml_qkT_ready, 1)
                    elif step == "att_s":
                        for j in range(NB):
                            pr = probs[i % 2][:, ROWS_AT[j]:ROWS_AT[j] + (j + 1) * P]
                            e.wait_ge(att_masked, i * NB + j + 1)
                            e.activation(pr, pr, ACT.Exp, scale=-1.0, bias=nmax[:, i, j:j + 1], accum_out=den[:, i, j:j + 1]).then_inc(att_probs, 1)
                    elif step == "ml_vo":
                        if i == 0:
                            e.wait_ge(vones_set, NB)
                        src = read(e, step, i)
                        e.copy(ml_v[:, i, :, 0:AD], src[:, 0:256].rearrange("p (h c) -> p h c", h=H))
                        e.activation(ml_o[:, i, :], src[:, 256:512], ACT.Sigmoid).then_inc(freed(step, i), 1)
                        e.drain()
                        e.sem_inc(ml_v_ready, 1)
                        e.sem_inc(ml_o_ready, 1)
                    elif step == "ml_s":
                        for j in range(NB):
                            st = strips[i % 2][:, TRI_AT[j]:TRI_AT[j] + TRI[j]]
                            e.wait_ge(ml_expo, i * NB + j + 1)
                            e.activation(st, st, ACT.Exp, bias=gcols[:, 0, j, i:i + 1]).then_inc(ml_weight, 1)
                    elif step == "ret_g":
                        e.activation(ret_gate[:, i, :], read(e, step, i)[:, :], ACT.Silu).then_inc(freed(step, i), 1)
                        e.drain()
                        e.sem_inc(ret_silu, 1)
                    elif step == "ml_norm":
                        e.wait_ge(var_ready, 2)
                        e.sqrt(rstd[:, :], rstd[:, :]).then_inc(std_ready, 1)
                    elif step == "mix_tr" :
                        src = read(e, step, i, 1).rearrange("p (k t) -> p k t", k=4)
                        e.copy(xT[:, 4:8, i * P:(i + 1) * P], src).then_inc(freed(step, i, 1), 1)
                        e.drain()
                        e.sem_inc(mixT_ready, 1)
                    elif step == "out":
                        e.wait_ge(var_ready, 3 + i)
                        e.sqrt(lnr[:, :], lnr[:, :]).then_inc(std_ready, 1)
                    elif step == "x1_tr":
                        for n in range(2):
                            src = read(e, step, i, n).rearrange("p (k t) -> p k t", k=4)
                            e.copy(xT[:, 4 * n:4 * n + 4, i * P:(i + 1) * P], src).then_inc(freed(step, i, n), 1)
                        e.drain()
                        e.sem_inc(x1T_ready, 1)
                    elif step == "first_q":
                        e.wait_ge(first_q_full, i + 1)
                        src = bank[4 + i % 2][:, 0:2 * P].rearrange("p (x t) -> p x t", x=2)
                        e.copy(qT[:, :, i * P:(i + 1) * P], src).then_inc(first_q_ready, 1)

                def queries():
                    for n in range(2):
                        e.copy(qT[:, n, :], bank[4 + n][:, :])
                    e.drain()
                    e.sem_inc(q_ready, 1)

                def choice(b):
                    e.activation(gexp[:, b, :], gexp[:, b, :], ACT.Exp, bias=neg_best[:, b:b + 1], accum_out=gsum[:, b:b + 1]).then_inc(gexp_ready, 1)

                for b in range(NB - 1):
                    e.wait_ge(chosen_rows, b + 1)
                    choice(b)
                for b in range(NB):
                    e.mul(acc[:, b, :], x[:, b, :], ALPHA).then_inc(acc_started, 1)

                def head(h, more):
                    for b in range(NB):
                        n = h * NB + b
                        e.wait_ge(u_free, n * TOPK + (UR + TOPK))
                        e.activation(act_d, dots[:, b % 2, :], ACT.Gelu).then_inc(gelu_done, 1)
                        if more or b == 0:
                            e.wait_ge(chosen_rows, n + NB)
                            choice((b + NB - 1) % NB)
                        if b == 0 and more:
                            e.wait_ge(q_full, h + 2)
                            queries()
                        if not more:
                            e.wait_ge(ple_full, b + 1)
                            if b > 0:
                                e.wait_ge(ple_added, b)
                            for m in range(2):
                                ins = e.activation(ple_s[:, m * 512:(m + 1) * 512], bank[4 + m][:, :], ACT.Sigmoid)
                            ins.then_inc(ple_gate, 1)
                        e.wait_ge(wgt_ready, n + 1)
                        for k in range(TOPK):
                            e.wait_ge(v_free, n * TOPK + (VR + k - DR + 1))
                            e.activation(diag[:, k % DR, :], ident, ACT.Copy, scale=wgt[:, b % 2, k:k + 1]).then_inc(diag_ready, 1)

                with e.Fori(0, PH - 1) as h:
                    head(h, True)
                head(PH - 1, False)
                for b in range(NB):
                    e.wait_ge(var_ready, 2 + NB + b + 1)
                    e.sqrt(lnr[:, :], lnr[:, :]).then_inc(std_ready, 1)
                end_layer(e, l)

        @block.vector
        def _(e):
            e.wait_ge(keep_in, 16)

            def head_norm(at_col, width, kind):
                for h in range(H):
                    for b in range(NB):
                        e.bn_stats(stats[:, h * NB + b, :], acc[:, b, at_col + h * width:at_col + (h + 1) * width])
                e.drain()
                for n in range(H * NB):
                    e.bn_aggr(mv[:, n, :], stats[:, n, :])
                e.drain()
                e.tensor_scalar(rstd[:, :], mv[:, :, 1], EPS, None, ALU.add).then_inc(var_ready, 1)
                e.wait_ge(std_ready, 1 + kind)
                e.reciprocal(rstd[:, :], rstd[:, :])
                e.drain()
                for h in range(H):
                    for b in range(NB):
                        n = h * NB + b
                        v = acc[:, b, at_col + h * width:at_col + (h + 1) * width]
                        e.tensor_scalar(v, v, mv[:, n, 0:1], rstd[:, n:n + 1], ALU.subtract, ALU.mult)

            def layer_norm(rows_, g, count, done):
                for n in range(2):
                    e.bn_stats(lnst[:, n, :], rows_[:, n * 512:(n + 1) * 512])
                e.drain()
                e.bn_aggr(lnmv[:, :], lnst[:, :, :].rearrange("p n c -> p (n c)"))
                e.drain()
                e.tensor_scalar(lnr[:, :], lnmv[:, 1:2], EPS, None, ALU.add).then_inc(var_ready, 1)
                e.wait_ge(std_ready, count)
                e.reciprocal(lnr[:, :], lnr[:, :])
                e.drain()
                e.tensor_scalar(rows_, rows_, lnmv[:, 0:1], lnr[:, 0:1], ALU.subtract, ALU.mult)
                e.drain()
                e.tensor_tensor(rows_, rows_, ln[:, g, :], ALU.mult)
                e.drain()
                return e.tensor_tensor(done, rows_, ln[:, g + 1, :], ALU.add)

            e.memset(layer_row[:, :], 0.0)
            e.drain()
            with e.Fori(0, DEPTH) as l:
                def choose(b):
                    sc = bank[6 + b % 2][:, (b // 2) * 256:(b // 2) * 256 + 256].rearrange("p (x n) -> p x n", x=2)
                    for s in range(2):
                        r = rest[:, s * NKEYS:(s + 1) * NKEYS]
                        e.max(top[:, s, 0:8], sc[:, s, :])
                        e.drain()
                        e.max_index(topi[:, s, 0:8], top[:, s, 0:8], sc[:, s, :])
                        e.match_replace(r, top[:, s, 0:8], sc[:, s, :], LOWEST)
                        e.drain()
                        e.max(top[:, s, 8:16], r)
                        e.drain()
                        e.max_index(topi[:, s, 8:16], top[:, s, 8:16], r)
                    e.drain()
                    pr = pairs.rearrange("p (i j) -> p i j", i=TOPK)
                    e.tensor_tensor(pr, top[:, 0, :].unsqueeze(2).to_broadcast([P, TOPK, TOPK]),
                                    top[:, 1:2, :].to_broadcast([P, TOPK, TOPK]), ALU.add)
                    e.tensor_copy(topi_f, topi[:, :, :])
                    e.drain()
                    e.max(best[:, 0:8], pairs)
                    e.drain()
                    e.max_index(pos[:, 0:8], best[:, 0:8], pairs)
                    e.match_replace(pairs2, best[:, 0:8], pairs, LOWEST)
                    e.drain()
                    e.max(best[:, 8:16], pairs2)
                    e.drain()
                    e.max_index(pos[:, 8:16], best[:, 8:16], pairs2)
                    e.tensor_copy(gexp[:, b, :], best)
                    e.tensor_scalar(neg_best[:, b:b + 1], best[:, 0:1], -1.0, None, ALU.mult)
                    e.drain()
                    e.tensor_scalar(rank[:, 0, :], pos[:, :], 4, None, ALU.logical_shift_right)
                    e.tensor_scalar(rank[:, 1, :], pos[:, :], 15, None, ALU.bitwise_and)
                    e.drain()
                    e.tensor_copy(rank_f, rank[:, :, :])
                    e.drain()
                    oh = onehot.rearrange("p (x k r) -> p x k r", x=2, k=TOPK)
                    it = iota16.unsqueeze(1).to_broadcast([P, TOPK, TOPK])
                    for s in range(2):
                        e.tensor_tensor(oh[:, s], rank_f[:, s, :].unsqueeze(2).to_broadcast([P, TOPK, TOPK]), it, ALU.is_equal)
                    e.drain()
                    for s in range(2):
                        e.tensor_tensor(oh[:, s], oh[:, s], topi_f[:, s:s + 1, :].to_broadcast([P, TOPK, TOPK]), ALU.mult)
                    e.drain()
                    e.tensor_reduce(chosen, oh, AX_X, ALU.add)
                    e.drain()
                    e.scalar_tensor_tensor(row_f, chosen[:, 0, :], float(NKEYS), chosen[:, 1, :], ALU.mult, ALU.add)
                    e.drain()
                    e.tensor_scalar(rows[:, b, :], row_f, layer_row[:, 0:1], None, ALU.add).then_inc(chosen_rows, 1)
                    e.drain()

                def dot_products(h, b):
                    n = h * NB + b
                    for k in range(TOPK):
                        s = k % UR
                        e.wait_ge(u_in[s], (l * (PH * NB) + n) * (16 * TOPK // UR) + 16 * (k // UR + 1))
                        e.tensor_tensor_reduce(urow[s], urow[s], x[:, b, :], 1.0, 0.0, ALU.mult, ALU.add, dots[:, b % 2, k:k + 1]).then_inc(u_free, 1)
                    e.drain()

                for step, i in MIXER_STEPS:
                    if step == "xt" and i % 2 == 1:
                        e.tensor_copy(xT[:, i, :], read(e, step, i)[:, :]).then_inc(freed(step, i), 1)
                        e.drain()
                        e.sem_inc(xT_ready, 1)
                    elif step == "gate":
                        if i == 0:
                            e.wait_ge(gate_w_in, 48)
                        dst = (gi, gf)[i]
                        e.tensor_scalar(dst, read(e, step, i)[0:H, :], gate_b[:, i:i + 1], None, ALU.add).then_inc(freed(step, i), 1)
                        if i == 1:
                            e.drain()
                            e.scalar_tensor_tensor(gt, gf, -1.0, gf, ALU.mult, ALU.max).then_inc(gate_abs, 1)
                    elif step == "ret_qk":
                        if i == 0:
                            e.wait_ge(tables_in, 16)
                        if i >= 2:
                            e.wait_ge(*step_done("ret_tr", i - 2))
                        src = read(e, step, i).rearrange("p (g x c) -> p g x c", g=2 * H, x=2)
                        r, rb = (t[i % 2].rearrange("p (g x c) -> p g x c", g=2 * H, x=2) for t in (rot, rot_b))
                        cos = ret_cos[:, i:i + 1, :].rearrange("p o (x c) -> p o x c", x=2).to_broadcast([P, 2 * H, 2, DK // 2])
                        e.tensor_tensor(r, src, cos, ALU.mult)
                        for half in range(2):
                            sin = ret_sin[:, i:i + 1, half * 32:half * 32 + 32].to_broadcast([P, 2 * H, DK // 2])
                            ins = e.tensor_tensor(rb[:, :, half, :], src[:, :, 1 - half, :], sin, ALU.mult)
                        ins.then_inc(freed(step, i), 1)
                        e.drain()
                        e.sem_inc(rope_terms, 1)
                    elif step == "att_qk" and i == 0:
                        e.wait_ge(gate_log, 1)
                        e.scalar_tensor_tensor(gf, gf, 0.0, gt, ALU.min, ALU.subtract)
                        e.drain()
                        e.memset(gt, 1.0)
                        e.drain()
                        e.tensor_tensor_scan(gB, gt, gf, 0.0, ALU.mult, ALU.add)
                        e.drain()
                        e.tensor_tensor(gu, gi, gB, ALU.subtract)
                        e.drain()
                        e.tensor_tensor_scan(gM, gu, gu, 0.0, ALU.max, ALU.max)
                        e.drain()
                        e.tensor_tensor(gB, gB, gM, ALU.add)
                        e.drain()
                        e.sem_inc(gates_ready, 1)
                    if step == "att_qk":
                        e.wait_ge(att_copied, i + 1)
                        rr = att_rows4[i].rearrange("p (g c) -> p g c", g=2 * H)
                        n = ROPE_HALF
                        ta, tb = (rope_a[:, s, :].rearrange("p (g c) -> p g c", g=2 * H) for s in range(2))
                        e.tensor_tensor(ta, rr[:, :, 0:2 * n], att_cos[:, i:i + 1, :].to_broadcast([P, 2 * H, 2 * n]), ALU.mult)
                        for half in range(2):
                            e.tensor_tensor(tb[:, :, half * n:half * n + n], rr[:, :, (1 - half) * n:(2 - half) * n],
                                            att_sin[:, i:i + 1, half * n:half * n + n].to_broadcast([P, 2 * H, n]), ALU.mult)
                        e.drain()
                        e.tensor_tensor(rr[:, :, 0:2 * n], ta, tb, ALU.add).then_inc(att_rotated, 1)
                        e.drain()
                    elif step == "ret_s":
                        if i >= 2:
                            e.wait_ge(*step_done("ret_pv", i - 2))
                        for j in range(NB):
                            st = strips[i % 2][:, TRI_AT[j]:TRI_AT[j] + TRI[j]]
                            src = read(e, step, i, j)
                            e.tensor_tensor(st, src[:, 0:TRI[j]], decay[:, i, 0:TRI[j]], ALU.mult).then_inc(freed(step, i, j), 1)
                        e.drain()
                        e.sem_inc(ret_strip, 1)
                    elif step == "att_tr":
                        src = read(e, step, i).rearrange("p (g t) -> p g t", g=4)
                        e.tensor_copy(att_qkT[:, :, i * P:(i + 1) * P], src).then_inc(freed(step, i), 1)
                        e.drain()
                        e.sem_inc(att_qkT_ready, 1)
                    elif step == "ret_norm":
                        e.wait_ge(ret_raw, H)
                        head_norm(0, DV, 0)
                        e.drain()
                        e.sem_inc(ret_normed, 1)
                    elif step == "gate_cols":
                        src = read(e, step, i)[:, 0:2 * NB * H].rearrange("p (x b h) -> p x b h", x=2, b=NB)
                        e.tensor_copy(gcols, src).then_inc(freed(step, i), 1)
                        e.drain()
                        e.sem_inc(gate_cols_ready, 1)
                    elif step == "ml_qk":
                        e.wait_ge(pad_filled, i + 1)
                        v = ml_qkT[:, i, :]
                        e.tensor_scalar(v, pads[i][:, 0:SEQ], convw[:, i, 0:1], None, ALU.mult)
                        for w in range(1, 4):
                            e.drain()
                            e.scalar_tensor_tensor(v, pads[i][:, w:w + SEQ], convw[:, i, w:w + 1], v, ALU.mult, ALU.add)
                        e.drain()
                        e.sem_inc(conv_done, 1)
                    elif step == "att_s":
                        if i >= 2:
                            e.wait_ge(*step_done("att_tp", i - 2, NB - 1))
                        for j in range(NB):
                            w = (j + 1) * P
                            pr = probs[i % 2][:, ROWS_AT[j]:ROWS_AT[j] + w]
                            src = read(e, step, i, j)
                            e.tensor_tensor_reduce(pr, src[:, 0:w], counts[:, SEQ - w:SEQ], -AD ** -0.5, -LOWEST, ALU.add, ALU.min, nmax[:, i, j:j + 1]).then_inc(freed(step, i, j), 1)
                            e.drain()
                            e.sem_inc(att_masked, 1)
                    elif step == "att_tp":
                        if i >= 2:
                            e.wait_ge(*step_done("att_pv", i - 2))
                        for j in range(NB):
                            w = (j + 1) * P
                            src = read(e, step, i, j)
                            e.tensor_copy(probsT[i % 2][:, ROWS_AT[j]:ROWS_AT[j] + w], src[:, 0:w]).then_inc(freed(step, i, j), 1)
                        e.drain()
                        e.sem_inc(att_probsT, 1)
                    elif step == "att_pv":
                        e.wait_ge(att_probs, NB * (i + 1))
                        e.reciprocal(rden, den[:, i, :])
                        e.drain()
                        src = read(e, step, i)[:, 0:NB * AD].rearrange("p (b c) -> p b c", b=NB)
                        c = H * DV + i * AD
                        e.tensor_tensor(acc[:, :, c:c + AD], src, rden.unsqueeze(2).to_broadcast([P, NB, AD]), ALU.mult).then_inc(freed(step, i), 1)
                        e.drain()
                        e.sem_inc(att_done, 1)
                    elif step == "ml_s":
                        if i >= 2:
                            e.wait_ge(*step_done("ml_pv", i - 2))
                        src = read(e, step, i, 0)
                        for j in range(NB):
                            st = strips[i % 2][:, TRI_AT[j]:TRI_AT[j] + TRI[j]]
                            ins = e.scalar_tensor_tensor(st, src[:, j * P:SEQ], -1.0, causal[:, 0:TRI[j]], ALU.mult, ALU.add)
                            ins.then_inc(ml_expo, 1)
                        e.drain()
                        e.sem_inc(freed(step, i, 0), 1)
                        for j in range(NB):
                            st = strips[i % 2][:, TRI_AT[j]:TRI_AT[j] + TRI[j]]
                            e.wait_ge(ml_weight, i * NB + j + 1)
                            e.scalar_tensor_tensor(st, read(e, step, i, 1 + j)[:, 0:TRI[j]], AD ** -0.5, st, ALU.mult, ALU.mult).then_inc(freed(step, i, 1 + j), 1)
                        e.drain()
                        e.sem_inc(ml_strip, 1)
                    elif step == "ml_pv":
                        src = read(e, step, i)[:, 0:NB * (AD + 1)].rearrange("p (b c) -> p b c", b=NB)
                        if i == 0:
                            e.wait_ge(gate_exp, 1)
                        e.tensor_copy(mden, src[:, :, AD])
                        e.drain()
                        e.scalar_tensor_tensor(mden, mden, -1.0, mden, ALU.mult, ALU.max)
                        e.drain()
                        e.tensor_tensor(mden, mden, gcols[:, 1, :, i], ALU.max)
                        e.drain()
                        e.reciprocal(mden, mden)
                        e.drain()
                        c = H * (DV + AD) + i * AD
                        e.tensor_tensor(acc[:, :, c:c + AD], src[:, :, 0:AD], mden.unsqueeze(2).to_broadcast([P, NB, AD]), ALU.mult).then_inc(freed(step, i), 1)
                        e.drain()
                    elif step == "ml_norm":
                        c = H * (DV + AD)
                        head_norm(c, AD, 1)
                        e.drain()
                        e.wait_ge(ml_o_scaled, NB)
                        for b in range(NB):
                            e.tensor_tensor(acc[:, b, c:], acc[:, b, c:], ml_o[:, b, :], ALU.mult).then_inc(mix_ml, 1)
                    elif step == "mix_tr":
                        src = read(e, step, i, 0).rearrange("p (k t) -> p k t", k=4)
                        e.tensor_copy(xT[:, 0:4, i * P:(i + 1) * P], src).then_inc(freed(step, i, 0), 1)
                        e.drain()
                        e.sem_inc(mixT_ready, 1)
                    elif step == "out":
                        if i == 0:
                            e.wait_ge(params_in, 80)
                            e.wait_ge(x_in, 16)
                        if i == NB - 1:
                            dot_products(0, 0)
                        for n in range(2):
                            v = x[:, i, n * 512:(n + 1) * 512]
                            e.scalar_tensor_tensor(v, v, ALPHA, read(e, step, i, n)[:, :], ALU.mult, ALU.add).then_inc(freed(step, i, n), 1)
                        e.drain()
                        layer_norm(x[:, i, :], 0, 3 + i, x[:, i, :]).then_inc(x1_ready, 1)
                        e.drain()
                    elif step == "first_q" and i < NB - 1:
                        if i == 0:
                            e.sem_inc(u_free, UR)
                        e.wait_ge(scored, i + 1)
                        choose(i)

                def add_y(n, b):
                    v = acc[:, b, :]
                    for m in range(2):
                        ins = e.tensor_tensor(v[:, m * 512:(m + 1) * 512], v[:, m * 512:(m + 1) * 512], bank[2 * (b % 2) + m][:, :], ALU.add)
                    ins.then_inc(y_added, 1)
                    e.drain()

                def head(h, more, add_first=True):
                    for b in range(NB):
                        n = h * NB + b
                        if b > 0 or add_first:
                            dot_products(h, b)
                        if more or b == 0:
                            c = (b + NB - 1) % NB
                            e.wait_ge(scored, h * NB + (NB if b == 0 else 2 * NB))
                            if b > 0 or add_first:
                                e.wait_ge(v_free, n * TOPK + VR)
                            e.sem_inc(held, 1)
                            choose(c)
                        e.wait_ge(gexp_ready, n + 1)
                        e.reciprocal(grec, gsum[:, b:b + 1])
                        e.drain()
                        e.wait_ge(gelu_done, n + 1)
                        e.scalar_tensor_tensor(wgt[:, b % 2, :], act_d, grec[:, 0:1], gexp[:, b, :], ALU.mult, ALU.mult).then_inc(wgt_ready, 1)
                        e.drain()
                        if b > 0 or add_first:
                            e.wait_ge(v_free, n * TOPK + VR)
                            add_y(n, (b + NB - 1) % NB)
                        if not more:
                            e.wait_ge(ple_gate, b + 1)
                            for m in range(2):
                                v = ple_s[:, m * 512:(m + 1) * 512]
                                e.tensor_tensor(v, v, bank[6 + m][:, :], ALU.mult)
                            e.drain()
                            v = acc[:, :, b * PC:(b + 1) * PC]
                            e.tensor_tensor(v, v, ple_s.rearrange("p (b c) -> p b c", b=NB), ALU.add).then_inc(ple_added, 1)
                            e.drain()

                e.wait_ge(acc_started, NB)
                head(0, True, add_first=False)
                with e.Fori(1, PH - 1) as h:
                    head(h, True)
                head(PH - 1, False)
                for b in range(NB):
                    if b == NB - 1:
                        e.wait_ge(v_free, PH * NB * TOPK + VR)
                        add_y(PH * NB, b)
                    layer_norm(acc[:, b, :], 2, 2 + NB + b + 1, x[:, b, :])
                    e.drain()
                e.tensor_scalar(layer_row[:, :], layer_row[:, :], float(EXPERTS), None, ALU.add)
                e.drain()
                end_layer(e, l)

        @block.tensor
        def _(e):
            e.wait_ge(keep_in, 16)
            e.wait_ge(x_in, 16)

            def project(step, i, w):
                wt, landed, count = weight(step)
                if i == 0:
                    e.wait_ge(landed, count)
                if (step, i) == ("ret_qk", 0):
                    e.wait_ge(xT_ready, KT)
                ps = fill(e, step, i)
                for k in range(KT):
                    ins = e.matmul(ps[:, 0:w], xT[:, k, i * P:(i + 1) * P], wt[:, k, :], start=(k == 0), stop=(k == KT - 1))
                ins.then_inc(filled(step, i), 1)

            def transposes(step, i, n, srcs):
                ps = fill(e, step, i, n)
                for m, src in enumerate(srcs):
                    ins = e.transpose(ps[:, m * P:(m + 1) * P], src, ident)
                ins.then_inc(filled(step, i, n), 1)

            def half(t, g, h, lo, hi):
                r = (h % 2) * 64
                return t[r:r + 64, g + h // 2, lo:hi]

            with e.Fori(0, DEPTH) as l:
                def query():
                    for n in range(2):
                        for k in range(KT):
                            ins = e.matmul(bank[4 + n][:, :], wq[:, k, n * P:(n + 1) * P], xT[:, k, :], start=(k == 0), stop=(k == KT - 1))
                    ins.then_inc(q_full, 1)

                def score(b):
                    for s in range(2):
                        c = (b // 2) * 256 + s * NKEYS
                        ins = e.matmul(bank[6 + b % 2][:, c:c + NKEYS], qT[:, s, b * P:(b + 1) * P], keys[:, s, :], start=True, stop=True)
                    ins.then_inc(scored, 1)

                for step, i in MIXER_STEPS:
                    if step == "xt":
                        transposes(step, i, 0, [x[:, b, i * P:(i + 1) * P] for b in range(NB)])
                    elif step == "gate":
                        if i == 0:
                            e.wait_ge(gate_w_in, 48)
                        ps = fill(e, step, i)
                        for k in range(KT):
                            ins = e.matmul(ps[0:H, :], gate_w[:, k, i * H:(i + 1) * H], xT[:, k, :], start=(k == 0), stop=(k == KT - 1))
                        ins.then_inc(filled(step, i), 1)
                    elif step in ("ret_qk", "ret_v", "att_qk", "att_v", "ml_vo", "ret_g"):
                        project(step, i, GROUPS[step][1])
                    elif step == "ml_qk":
                        wt, landed, count = weight(step)
                        if i == 0:
                            e.wait_ge(landed, count)
                        ps = fill(e, step, i)
                        for k in range(KT):
                            ins = e.matmul(ps[:, :], wt[:, k, i * P:(i + 1) * P], xT[:, k, :], start=(k == 0), stop=(k == KT - 1))
                        ins.then_inc(filled(step, i), 1)
                    elif step == "ret_tr":
                        e.wait_ge(rot_rows, i + 1)
                        transposes(step, i, 0, [rot[i % 2][:, m * P:(m + 1) * P] for m in range(4)])
                    elif step == "att_tr":
                        e.wait_ge(att_rotated, i + 1)
                        transposes(step, i, 0, [att_rows4[i][:, m * P:(m + 1) * P] for m in range(4)])
                    elif step == "ret_s":
                        e.wait_ge(ret_qkT_ready, NB)
                        for j in range(NB):
                            ps = fill(e, step, i, j)
                            e.matmul(ps[:, 0:TRI[j]], half(ret_qkT, 2, i, j * P, (j + 1) * P), half(ret_qkT, 0, i, j * P, SEQ)).then_inc(filled(step, i, j), 1)
                    elif step == "ret_pv":
                        e.wait_ge(ret_v_ready, NB)
                        e.wait_ge(ret_strip, i + 1)
                        ps = fill(e, step, i)
                        for j in range(NB):
                            for s in range(j + 1):
                                st = strips[i % 2][:, TRI_AT[s] + (j - s) * P:TRI_AT[s] + (j - s + 1) * P]
                                ins = e.matmul(ps[:, j * DV:(j + 1) * DV], st, ret_v[:, s, i * DV:(i + 1) * DV], start=(s == 0), stop=(s == j))
                        ins.then_inc(filled(step, i), 1)
                    elif step == "gate_cols":
                        e.wait_ge(gates_ready, 1)
                        ps = fill(e, step, i)
                        for m, g in enumerate((gu, gB)):
                            for b in range(NB):
                                c = (m * NB + b) * H
                                ins = e.transpose(ps[:, c:c + H], g[:, b * P:(b + 1) * P], ident[0:H, 0:H])
                        ins.then_inc(filled(step, i), 1)
                    elif step == "att_s":
                        e.wait_ge(att_qkT_ready, NB)
                        for j in range(NB):
                            ps = fill(e, step, i, j)
                            e.matmul(ps[:, 0:(j + 1) * P], half(att_qkT, 0, i, j * P, (j + 1) * P), half(att_qkT, 2, i, 0, (j + 1) * P)).then_inc(filled(step, i, j), 1)
                    elif step == "att_tp":
                        for j in range(NB):
                            e.wait_ge(att_probs, i * NB + j + 1)
                            transposes(step, i, j, [probs[i % 2][:, ROWS_AT[j] + s * P:ROWS_AT[j] + (s + 1) * P] for s in range(j + 1)])
                    elif step == "att_pv":
                        e.wait_ge(att_v_ready, NB)
                        e.wait_ge(att_probsT, i + 1)
                        ps = fill(e, step, i)
                        for j in range(NB):
                            for s in range(j + 1):
                                ins = e.matmul(ps[:, j * AD:(j + 1) * AD], probsT[i % 2][:, ROWS_AT[j] + s * P:ROWS_AT[j] + (s + 1) * P],
                                               att_v[:, s, i * AD:(i + 1) * AD], start=(s == 0), stop=(s == j))
                        ins.then_inc(filled(step, i), 1)
                    elif step == "ml_s":
                        ps = fill(e, step, i, 0)
                        e.matmul(ps[:, :], pick[0:H, i, :], gM).then_inc(filled(step, i, 0), 1)
                        e.wait_ge(ml_qkT_ready, 4)
                        for j in range(NB):
                            ps = fill(e, step, i, 1 + j)
                            e.matmul(ps[:, 0:TRI[j]], half(ml_qkT, 2, i, j * P, (j + 1) * P), half(ml_qkT, 0, i, j * P, SEQ)).then_inc(filled(step, i, 1 + j), 1)
                    elif step == "ml_pv":
                        e.wait_ge(ml_v_ready, NB)
                        e.wait_ge(ml_strip, i + 1)
                        ps = fill(e, step, i)
                        w = AD + 1
                        for j in range(NB):
                            for s in range(j + 1):
                                st = strips[i % 2][:, TRI_AT[s] + (j - s) * P:TRI_AT[s] + (j - s + 1) * P]
                                ins = e.matmul(ps[:, j * w:(j + 1) * w], st, ml_v[:, s, i, :], start=(s == 0), stop=(s == j))
                        ins.then_inc(filled(step, i), 1)
                    elif step == "mix_tr":
                        e.wait_ge(mix_ml, i + 1)
                        e.wait_ge(mix_ret, i + 1)
                        e.wait_ge(att_done, H)
                        for n in range(2):
                            transposes(step, i, n, [acc[:, i, (4 * n + m) * P:(4 * n + m + 1) * P] for m in range(4)])
                    elif step == "out":
                        e.wait_ge(mixT_ready, 2 * i + 2)
                        for n in range(2):
                            ps = fill(e, step, i, n)
                            for k in range(KT):
                                wt, landed, count = out_weight(k // 4)
                                if i == 0 and n == 0 and k % 4 == 0:
                                    e.wait_ge(landed, count)
                                ins = e.matmul(ps[:, :], xT[:, k, i * P:(i + 1) * P], wt[:, k % 4, n * 512:(n + 1) * 512], start=(k == 0), stop=(k == KT - 1))
                            ins.then_inc(filled(step, i, n), 1)
                    elif step == "x1_tr":
                        e.wait_ge(x1_ready, i + 1)
                        for n in range(2):
                            transposes(step, i, n, [x[:, i, (4 * n + m) * P:(4 * n + m + 1) * P] for m in range(4)])
                        if i == NB - 2:
                            e.drain()
                            e.sem_inc(v_free, VLATE)
                    elif step == "first_q":
                        e.wait_ge(x1T_ready, i + 1)
                        if i == 0:
                            e.sem_inc(v_free, VR - VLATE)
                            e.wait_ge(wq_in, 16)
                        if i >= 2:
                            e.wait_ge(first_q_ready, i - 1)
                        for n in range(2):
                            for k in range(KT):
                                ins = e.matmul(bank[4 + i % 2][:, n * P:(n + 1) * P], wq[:, k, n * P:(n + 1) * P], xT[:, k, i * P:(i + 1) * P], start=(k == 0), stop=(k == KT - 1))
                        ins.then_inc(first_q_full, 1)
                        if i == NB - 1:
                            e.drain()
                            e.sem_inc(q_full, 1)
                        e.wait_ge(first_q_ready, i + 1)
                        if i == 0:
                            e.wait_ge(keys_in, 16)
                        if i >= 2:
                            e.wait_ge(chosen_rows, i - 1)
                        score(i)

                def head(h, more, first_head=False):
                    if more:
                        e.wait_ge(wq_in, h * 16 + 32)
                        if not first_head:
                            e.wait_ge(q_ready, h)
                        query()
                    for b in range(NB):
                        n = h * NB + b
                        if not more:
                            e.wait_ge(ple_in, 16 * (2 + 2 * (b + 1)))
                            if b == 0:
                                e.wait_ge(chosen_rows, PH * NB)
                            else:
                                e.wait_ge(ple_added, b)
                            for t in range(NB):
                                g = bank[4 + t // 2][:, (t % 2) * PC:(t % 2 + 1) * PC]
                                for k in range(KT):
                                    e.matmul(g, xT[:, k, t * P:(t + 1) * P], wq[:, k, :], start=(k == 0), stop=False)
                                e.matmul(g, ones[0:1, :], bg[0:1, b * PC:(b + 1) * PC], start=False, stop=True)
                                v = bank[6 + t // 2][:, (t % 2) * PC:(t % 2 + 1) * PC]
                                for k in range(2):
                                    ins = e.matmul(v, pT[:, k, t * P:(t + 1) * P], wp[:, k, :], start=(k == 0), stop=(k == 1))
                            ins.then_inc(ple_full, 1)
                        if not (first_head and b < 2):
                            e.wait_ge(y_added, h * NB + (b - 1)) if first_head or b > 0 else e.wait_ge(y_added, h * NB - 1)
                        for k in range(TOPK):
                            e.wait_ge(v_in[k], (l * (PH * NB) + n) * 16 + 16)
                            e.wait_ge(diag_ready, n * TOPK + (k + 1))
                            for m in range(2):
                                ins = e.matmul(bank[2 * (b % 2) + m][:, :], diag[:, k % DR, :], vrow[k][:, m * 512:(m + 1) * 512], start=(k == 0), stop=(k == TOPK - 1))
                            ins.then_inc(v_free, 1)
                        if b == 0 and more:
                            e.wait_ge(q_ready, h + 1)
                            e.wait_ge(keys_in, h * 16 + 32)
                            e.wait_ge(chosen_rows, h * NB + NB)
                            for c in range(NB):
                                score(c)

                head(0, True, first_head=True)
                with e.Fori(1, PH - 1) as h:
                    head(h, True)
                head(PH - 1, False)
                end_layer(e, l)


def kernel(**inputs):
    import concourse.bacc as _bacc
    from concourse.bass_utils import run_bass_kernel_spmd as _run

    i = {n: np.asarray(v) for n, v in inputs.items()}
    keep, mixer = tables()
    c = np.ascontiguousarray
    arrays = {
        "keep": keep,
        "mixer": mixer,
        "x": c(i["x"][0]),
        "pT": c(i["p"][:, 0].transpose(0, 2, 1)),
        "w_in": c(i["w_in"]),
        "conv_w": c(i["conv_w"].reshape(DEPTH, 4, 4, P).transpose(0, 3, 2, 1).reshape(DEPTH, P, 16)),
        "gate_b": c(i["b_if"].reshape(DEPTH, 2, H).transpose(0, 2, 1)),
        "norm_g": c(np.concatenate([i["ret_norm_g"], i["mlstm_norm_g"]], 1)),
        "w_out": c(i["w_out"]),
        "ln": c(np.stack([i["ln1_g"], i["ln1_b"], i["ln2_g"], i["ln2_b"]], 1)),
        "peer_wq": c(i["peer_wq"]),
        "keysT": c(i["peer_keys"].transpose(0, 1, 4, 2, 3)),
        "peer_u": c(i["peer_u"].reshape(DEPTH * EXPERTS, D)),
        "peer_v": c(i["peer_v"].reshape(DEPTH * EXPERTS, D)),
        "ple_wg": c(i["ple_wg"]),
        "ple_bg": c(i["ple_bg"]),
        "ple_wp": c(i["ple_wp"]),
    }
    nc = _bacc.Bacc("TRN2", target_bir_lowering=False, num_devices=1)
    aps = {n: nc.dram_tensor(f"in_{n}", v.shape, F32, kind="ExternalInput").ap() for n, v in arrays.items()}
    out = nc.dram_tensor("out", (SEQ, D), F32, kind="ExternalOutput").ap()
    build(nc, aps, out)
    r = _run(nc, [{f"in_{n}": v for n, v in arrays.items()}], core_ids=[0])
    return r.results[0]["out"].reshape(1, SEQ, D)
```

```python
import math
from contextlib import ExitStack

import numpy as np
import concourse.bass as bass
from concourse import mybir

F32 = mybir.dt.float32
U32 = mybir.dt.uint32
ALU = mybir.AluOpType
ACT = mybir.ActivationFunctionType
AX_X = mybir.AxisListType.X

P = 128
DEPTH, SEQ, D = 2, 512, 1024
NB = SEQ // P
KT = D // P
H = 4
DK, DV = 64, 128
AD = 64
ROPE_HALF = AD // 4 // 2
GROUPS = {
    "ret_qk": (0, 512), "ret_v": (512, 512), "ret_g": (1024, 512), "att_qk": (1536, 512),
    "att_v": (2048, 256), "ml_qk": (2304, 512), "ml_vo": (2816, 512),
}
GATE_COL = 3328
FROW = 32
W_ORDER = ["ret_qk", "ret_v", "att_qk", "att_v", "ml_qk", "ml_vo", "ret_g"]
PH, NKEYS, QD, TOPK = 8, 128, 256, 16
EXPERTS = NKEYS * NKEYS
PLE = 256
ALPHA = (2 * DEPTH) ** 0.25
EPS = 1e-5
NEG = -1e30
LOWEST = -3.0e38
TRI = [(NB - i) * P for i in range(NB)]
TRI_AT = [sum(TRI[:i]) for i in range(NB)]
STRIPS = sum(TRI)
ROWS_AT = [sum((i + 1) * P for i in range(j)) for j in range(NB)]
TRI_BANKS = (((0, 0),), ((1, 0), (3, TRI[1])), ((2, 0),))
ROW_BANKS = (((0, 0), (2, P)), ((1, 0),), ((3, 0),))
UR, VR, DR = 8, TOPK, 4
PC = D // NB

MIXER_STEPS = (
    [("xt", k) for k in range(KT)]
    + [("ret_qk", 0), ("ret_qk", 1), ("gate", 0), ("ret_tr", 0), ("ret_qk", 2),
       ("ret_tr", 1), ("ret_qk", 3), ("ret_v", 0), ("ret_tr", 2), ("ret_v", 1), ("ret_tr", 3),
       ("ret_v", 2), ("ret_v", 3)]
    + [("att_qk", 0), ("ret_s", 0), ("att_qk", 1), ("ret_pv", 0), ("ret_s", 1), ("att_qk", 2),
       ("ret_pv", 1), ("ret_s", 2), ("att_qk", 3), ("ret_pv", 2), ("ret_s", 3),
       ("att_v", 0), ("ret_pv", 3), ("att_tr", 0), ("att_tr", 1), ("att_v", 1), ("ret_norm", 0),
       ("att_tr", 2), ("att_tr", 3), ("att_v", 2), ("att_v", 3), ("gate_cols", 0),
       ("ml_qk", 0), ("att_s", 0), ("ml_qk", 1), ("att_tp", 0), ("att_s", 1),
       ("ml_qk", 2), ("att_pv", 0), ("att_tp", 1), ("att_s", 2),
       ("ml_qk", 3), ("att_pv", 1), ("att_tp", 2), ("att_s", 3),
       ("ml_vo", 0), ("att_pv", 2), ("att_tp", 3), ("ml_vo", 1), ("att_pv", 3), ("ml_s", 0),
       ("ml_vo", 2), ("ml_vo", 3), ("ml_pv", 0), ("ml_s", 1),
       ("ret_g", 0), ("ml_pv", 1), ("ml_s", 2), ("ret_g", 1), ("ml_pv", 2), ("ml_s", 3),
       ("ret_g", 2), ("ml_pv", 3), ("ml_norm", 0), ("ret_g", 3)]
    + [("mix_tr", b) for b in range(NB)]
    + [("out", 0), ("out", 1), ("out", 2), ("x1_tr", 0), ("first_q", 0), ("out", 3), ("out", 4),
       ("x1_tr", 1), ("out", 5), ("first_q", 1), ("out", 6), ("out", 7), ("x1_tr", 2), ("first_q", 2),
       ("x1_tr", 3), ("first_q", 3)]
)
BANKS_OF = {
    "xt": (0, 1), "gate": (0, 1), "ret_qk": (0, 1), "ret_v": (0, 1), "att_qk": (0, 1), "att_v": (0, 1),
    "ml_qk": (0, 1), "ml_vo": (0, 1), "ret_g": (0, 1), "mix_tr": (0, 2), "out": (0, 1), "x1_tr": (0, 2),
    "ret_tr": (1, 1), "ret_s": (1, 3), "ret_pv": (1, 1), "att_tr": (1, 1), "att_s": (1, 3),
    "att_tp": (0, 3), "att_pv": (1, 1), "gate_cols": (1, 1), "ml_s": (1, 4), "ml_pv": (1, 1),
}


def bank_turns():
    used, turns = [0, 0], {}
    for step, i in MIXER_STEPS:
        ring, n = BANKS_OF.get(step, (0, 0))
        for j in range(n):
            turns[step, i, j] = (4 * ring + used[ring] % 4, used[ring] // 4 + 1)
            used[ring] += 1
    return turns


def tables():
    pos = np.arange(SEQ, dtype=np.float32)

    def rope(half, theta):
        inv = np.float32(theta) ** (-np.arange(half, dtype=np.float32) / np.float32(half))
        ang = pos[:, None] * inv[None, :]
        c, s = np.cos(ang), np.sin(ang)
        lay = lambda t: t.reshape(NB, P, 2 * half).transpose(1, 0, 2).reshape(P, -1)
        return lay(np.concatenate([c, c], 1)), lay(np.concatenate([-s, s], 1))

    row, col = np.arange(P)[:, None], np.arange(SEQ)[None, :]
    after = col - row
    decay = []
    for h in range(H):
        lg = math.log(1.0 - 2.0 ** (-5.0 - h))
        decay.append(np.where(after >= 0, np.exp(lg * np.maximum(after, 0)), 0.0) * DK ** -0.5)
    dist = (SEQ - P) + row - col
    seen = (dist >= 0) * ((dist <= P).astype(int) + (dist % 4 == 0) + (dist % 16 == 0))
    counts = np.where(seen > 0, np.log(np.maximum(seen, 1)), NEG) * AD ** 0.5
    causal = np.where(after >= 0, 0.0, NEG)
    pick = np.zeros((P, H, P))
    for h in range(H):
        pick[h, h] = 1.0
    f = lambda *t: np.concatenate([np.asarray(a, np.float32).reshape(P, -1) for a in t], 1)
    keep = f(np.eye(P), np.ones((P, P)), np.tile(np.arange(TOPK), (P, 1)))
    mixer = f(np.stack(decay, 1), counts, causal, *rope(DK // 2, 10000.0), *rope(ROPE_HALF, 500000.0),
              pick)
    return keep, mixer


def build(nc, a, out):
    turns = bank_turns()
    keep_w, mixer_w = a["keep"].shape[1], a["mixer"].shape[1]
    with ExitStack() as ctx:
        def sb(name, shape, dt=F32):
            return ctx.enter_context(nc.sbuf_tensor(name, shape, dt))

        def sem(name):
            return ctx.enter_context(nc.semaphore(name))

        keep = sb("keep", [P, keep_w])
        ident, ones, iota16 = keep[:, 0:P], keep[:, P:2 * P], keep[:, 2 * P:2 * P + TOPK]
        x = sb("x", [P, NB, D])
        xT = sb("xT", [P, KT, SEQ])
        acc = sb("acc", [P, NB, D])
        ln = sb("ln", [P, 4, D])
        normg = sb("normg", [P, H * DV + H * AD])
        layer_row = sb("layer_row", [P, 1])
        convw = sb("convw", [P, 4, 4])
        gate_b = sb("gate_b", [FROW + H, 1])
        gate_w = sb("gate_w", [P, KT, FROW + H])
        stats = sb("stats", [P, 16, 6])
        mv = sb("mv", [P, 16, 2])
        rstd = sb("rstd", [P, 16])

        ARENA = 34816
        arena = sb("arena", [P, ARENA])
        at = [0]

        def take(n):
            at[0] += n
            assert at[0] <= ARENA, at[0]
            return arena[:, at[0] - n:at[0]]

        WB = KT * 512
        wbuf = [take(WB) for _ in range(2)]
        mixt = take(mixer_w)
        o = [0]

        def part(n):
            o[0] += n
            return mixt[:, o[0] - n:o[0]]

        decay = part(H * SEQ).rearrange("p (h t) -> p h t", h=H)
        counts, causal = part(SEQ), part(SEQ)
        ret_cos, ret_sin = (part(NB * DK).rearrange("p (b d) -> p b d", b=NB) for _ in range(2))
        att_cos, att_sin = (part(NB * 2 * ROPE_HALF).rearrange("p (b d) -> p b d", b=NB) for _ in range(2))
        pick = part(H * P).rearrange("p (h t) -> p h t", h=H)
        ret_qkT = take(4 * SEQ).rearrange("p (g t) -> p g t", g=4)
        ret_v = take(NB * 512).rearrange("p (b c) -> p b c", b=NB)
        att_qkT = take(4 * SEQ).rearrange("p (g t) -> p g t", g=4)
        att_v = take(NB * 256).rearrange("p (b c) -> p b c", b=NB)
        ml_qkT = take(4 * SEQ).rearrange("p (g t) -> p g t", g=4)
        ml_v = take(NB * H * (AD + 1)).rearrange("p (b h c) -> p b h c", b=NB, h=H)
        ml_o = take(NB * 256).rearrange("p (b c) -> p b c", b=NB)
        ret_gate = take(NB * 512).rearrange("p (b c) -> p b c", b=NB)
        strips = [take(STRIPS) for _ in range(2)]
        probs = [take(STRIPS) for _ in range(2)]
        probsT = [take(STRIPS) for _ in range(2)]
        gates = take(2 * SEQ).rearrange("p (g t) -> p g t", g=2)
        gu, gM = (gates[0:H, n, :] for n in range(2))
        gates_if, gi, gf = ret_gate[0:FROW + H, 0, :], ret_gate[0:H, 0, :], ret_gate[FROW:FROW + H, 0, :]
        gt, gone, gB = ret_gate[FROW:FROW + H, 1, :], ret_gate[FROW:FROW + H, 2, :], ret_gate[0:H, 3, :]
        gcols = take(2 * NB * H).rearrange("p (x b h) -> p x b h", x=2, b=NB)
        small = take(64)
        nmax = small[:, 0:16].rearrange("p (h j) -> p h j", h=H)
        den = small[:, 16:32].rearrange("p (h j) -> p h j", h=H)
        rden = small[:, 32:36]
        mden = small[:, 36:40]
        rope_a = take(2 * 8 * 2 * ROPE_HALF).rearrange("p (s c) -> p s c", s=2)
        rot = [probs[0][:, 0:512], probs[1][:, 0:512]]
        rot_b = [probsT[0][:, 0:512], probsT[1][:, 0:512]]
        att_rows4 = [probs[n // 2][:, (n % 2) * 512:(n % 2 + 1) * 512] for n in range(NB)]
        PADW = SEQ + 3
        pads = [strips[n // 2][:, (n % 2) * PADW:(n % 2 + 1) * PADW] for n in range(4)]
        mixer_words = at[0]

        at[0] = 0
        VLATE = 2 * WB // D
        vlate = take(VLATE * D).rearrange("p (s d) -> p s d", s=VLATE)
        vearly = take((VR - VLATE) * D).rearrange("p (s d) -> p s d", s=VR - VLATE)
        vrow = [vearly[:, s, :] for s in range(VR - VLATE)] + [vlate[:, s, :] for s in range(VLATE)]
        uring = take(UR * D).rearrange("p (s d) -> p s d", s=UR)
        urow = [uring[:, s, :] for s in range(UR)]
        wq = take(KT * QD).rearrange("p (k c) -> p k c", k=KT)
        keys = take(2 * NKEYS).rearrange("p (x n) -> p x n", x=2)
        qT = take(2 * SEQ).rearrange("p (x t) -> p x t", x=2)
        diag = take(DR * P).rearrange("p (s c) -> p s c", s=DR)
        pT = take(2 * SEQ).rearrange("p (k t) -> p k t", k=2)
        wp = take(2 * PC).rearrange("p (k c) -> p k c", k=2)
        bg = take(D)
        ple_s = take(NB * PC)
        rest = take(256)
        pairs = take(256)
        pairs2 = take(256)
        onehot = take(2 * TOPK * TOPK)
        top = take(2 * TOPK).rearrange("p (x k) -> p x k", x=2)
        topi_f = take(2 * TOPK).rearrange("p (x k) -> p x k", x=2)
        best = take(TOPK)
        rank_f = take(2 * TOPK).rearrange("p (x k) -> p x k", x=2)
        chosen = take(2 * TOPK).rearrange("p (x k) -> p x k", x=2)
        row_f = take(TOPK)
        neg_best = take(NB)
        gsum = take(NB)
        grec = take(1)
        gexp = take(NB * TOPK).rearrange("p (b k) -> p b k", b=NB)
        dots = take(2 * TOPK).rearrange("p (s k) -> p s k", s=2)
        act_d = take(TOPK)
        wgt = take(2 * TOPK).rearrange("p (s k) -> p s k", s=2)
        topi = sb("topi", [P, 2, TOPK], U32)
        pos = sb("pos", [P, TOPK], U32)
        rank = sb("rank", [P, 2, TOPK], U32)
        rows = sb("rows", [P, NB, TOPK], U32)

        bank = [ctx.enter_context(nc.psum_tensor(f"bank{n}", [P, 512], F32)) for n in range(8)]

        first = sem("layer_sems_first")
        bank_full = [sem(f"bank_full{n}") for n in range(8)]
        bank_free = [sem(f"bank_free{n}") for n in range(8)]
        w_in_sem = [sem(f"w_landed{n}") for n in range(2)]
        tables_in, params_in, gate_w_in = sem("tables_in"), sem("params_in"), sem("gate_w_in")
        pads_clear, vones_set = sem("pads_clear"), sem("vones_set")
        xT_ready = sem("xT_ready")
        rope_terms, rot_rows, att_copied, att_rotated = (sem(n) for n in ("rope_terms", "rot_rows", "att_copied", "att_rotated"))
        ret_qkT_ready, ret_v_ready, att_qkT_ready, att_v_ready = (sem(n) for n in ("ret_qkT_ready", "ret_v_ready", "att_qkT_ready", "att_v_ready"))
        pad_filled, conv_done, ml_qkT_ready, ml_v_ready, ml_o_ready, ml_o_scaled = (sem(n) for n in ("pad_filled", "conv_done", "ml_qkT_ready", "ml_v_ready", "ml_o_ready", "ml_o_scaled"))
        gate_abs, gate_log, gates_ready, gate_cols_ready, gate_exp = (sem(n) for n in ("gate_abs", "gate_log", "gates_ready", "gate_cols_ready", "gate_exp"))
        ret_strip, ret_raw, var_ready, std_ready, ret_normed = (sem(n) for n in ("ret_strip", "ret_raw", "var_ready", "std_ready", "ret_normed"))
        att_masked, att_probs, att_probsT, att_done = (sem(n) for n in ("att_masked", "att_probs", "att_probsT", "att_done"))
        ml_expo, ml_weight, ml_strip, mix_ml = (sem(n) for n in ("ml_expo", "ml_weight", "ml_strip", "mix_ml"))
        ret_silu, mix_ret = sem("ret_silu"), sem("mix_ret")
        mixT_ready, x1_ready, x1T_ready = sem("mixT_ready"), sem("x1_ready"), sem("x1T_ready")
        acc_started = sem("acc_started")
        wq_in, keys_in = sem("wq_in"), sem("keys_in")
        pT_in, ple_wg_in, ple_wp_in = sem("pT_in"), sem("ple_wg_in"), sem("ple_wp_in")
        q_full, q_ready, scored, chosen_rows, gexp_ready = (sem(n) for n in ("q_full", "q_ready", "scored", "chosen_rows", "gexp_ready"))
        u_free, v_free = sem("u_free"), sem("v_free")
        first_q_full, first_q_ready = sem("first_q_full"), sem("first_q_ready")
        gelu_done, wgt_ready, diag_ready, y_added = (sem(n) for n in ("gelu_done", "wgt_ready", "diag_ready", "y_added"))
        ple_gate_full, ple_value_full = sem("ple_gate_full"), sem("ple_value_full")
        ple_gate, ple_added = sem("ple_gate"), sem("ple_added")
        held = sem("held")
        arrived = sem("arrived")
        u_in = [sem(f"u_in{n}") for n in range(UR)]
        v_in = [sem(f"v_in{n}") for n in range(VR)]
        layer_done = sem("layer_done")
        passed = sem("passed")
        keep_in, x_in, out_done = sem("keep_in"), sem("x_in"), sem("out_done")

        def number(s):
            return s.num if hasattr(s, "num") else int(s)

        layer_range = range(number(first), number(arrived) + 1)
        assert not any(number(s) in layer_range for s in (*u_in, *v_in, layer_done, passed, keep_in, x_in, out_done))

        flat = {n: a[n].rearrange("l r c -> (l r) c") for n in ("w_in", "w_out", "peer_wq", "ple_wg", "ple_wp", "pT")}

        def fill(e, step, i, n=0):
            b, turn = turns[step, i, n]
            if turn > 1:
                e.wait_ge(bank_free[b], turn - 1)
            return bank[b]

        def filled(step, i, n=0):
            return bank_full[turns[step, i, n][0]]

        def step_done(step, i, n=0):
            b, turn = turns[step, i, n]
            return bank_full[b], turn

        def read(e, step, i, n=0):
            b, turn = turns[step, i, n]
            e.wait_ge(bank_full[b], turn)
            return bank[b]

        def freed(step, i, n=0):
            return bank_free[turns[step, i, n][0]]

        def end_layer(e, layer, lead=False):
            e.sem_inc(arrived, 1)
            if lead:
                e.wait_ge(arrived, 5)
                e.sem_clear(layer_range)
                e.sem_inc(layer_done, 1)
            e.wait_ge(layer_done, layer + 1)
            e.sem_inc(passed, 1)

        def group_load(n):
            buf = wbuf[n % 2]
            if n < len(W_ORDER):
                c, w = GROUPS[W_ORDER[n]]
                return "w_in", c, w, 0, KT, buf[:, 0:KT * w].rearrange("p (k c) -> p k c", k=KT)
            half = n - len(W_ORDER)
            return "w_out", 0, D, half * KT // 2, KT // 2, buf.rearrange("p (k c) -> p k c", k=KT // 2)

        def weight(name):
            n = W_ORDER.index(name)
            w = GROUPS[name][1]
            return wbuf[n % 2][:, 0:KT * w].rearrange("p (k c) -> p k c", k=KT), w_in_sem[n % 2], 16 * (n // 2 + 1)

        def out_weight(half):
            n = len(W_ORDER) + half
            return wbuf[n % 2].rearrange("p (k c) -> p k c", k=KT // 2), w_in_sem[n % 2], 16 * (n // 2 + 1)

        def choices(b, more, first_head):
            if first_head:
                return ((), (NB - 1,), (0, 1), (2,))[b]
            if b == 0:
                return (NB - 1,)
            return (b - 1,) if more else ()

        block = ctx.enter_context(nc.Block())

        @block.sync
        def _(e):
            e.dma_start(keep[:, :], a["keep"]).then_inc(keep_in, 16)
            xr = a["x"].rearrange("(b p) d -> p b d", p=P)
            e.dma_start(x[:, :, :], xr).then_inc(x_in, 16)
            with e.Fori(0, DEPTH) as l:
                for n in range(len(W_ORDER) + 2):
                    name, c, w, k0, nk, dst = group_load(n)
                    if n >= 2:
                        b, turn = turns[W_ORDER[n - 2], NB - 1, 0]
                        e.wait_ge(bank_full[b], turn)
                    src = flat[name][bass.ds(l * D + k0 * P, nk * P), c:c + w]
                    e.dma_start(dst, src.rearrange("(k p) c -> p k c", p=P)).then_inc(w_in_sem[n % 2], 16)
                    if n == 1:
                        e.dma_start(mixt, a["mixer"]).then_inc(tables_in, 16)
                    if n == 3:
                        for n in range(4):
                            e.dma_start(ln[:, n, :], a["ln"].rearrange("l n d -> (l n) d")[bass.ds(l * 4 + n, 1), :].to_broadcast([P, D])).then_inc(params_in, 16)
                        e.dma_start(normg[:, :], a["norm_g"][bass.ds(l, 1), :].to_broadcast([P, H * DV + H * AD])).then_inc(params_in, 16)
                e.wait_ge(mix_ml, NB)
                e.wait_ge(mix_ret, NB)
                e.dma_start(wq, flat["peer_wq"][bass.ds(l * D, D), 0:QD].rearrange("(k p) c -> p k c", p=P)).then_inc(wq_in, 16)
                keys_at = a["keysT"].rearrange("l h c x n -> (l h c) (x n)")
                e.dma_start(keys.rearrange("p x n -> p (x n)"), keys_at[bass.ds(l * (PH * P), P), :]).then_inc(keys_in, 16)
                e.dma_start(pT, flat["pT"][bass.ds(l * PLE, PLE), :].rearrange("(k p) t -> p k t", p=P)).then_inc(pT_in, 16)
                e.dma_start(bg[0:1, :], a["ple_bg"][bass.ds(l, 1), :]).then_inc(pT_in, 16)
                wq_cols = flat["peer_wq"].rearrange("r (h c) -> h r c", h=PH)
                with e.Fori(0, PH - 1) as h:
                    e.wait_ge(q_full, h + 1)
                    e.dma_start(wq, wq_cols[bass.ds(h + 1, 1), bass.ds(l * D, D), :].rearrange("o (k p) c -> p (o k) c", p=P)).then_inc(wq_in, 16)
                    e.wait_ge(scored, h * NB + NB)
                    e.dma_start(keys.rearrange("p x n -> p (x n)"), keys_at[bass.ds((l * PH + h + 1) * P, P), :]).then_inc(keys_in, 16)
                for c in range(NB):
                    e.wait_ge(q_full, PH) if c == 0 else e.wait_ge(ple_gate_full, c)
                    e.dma_start(wq, flat["ple_wg"][bass.ds(l * D, D), c * PC:(c + 1) * PC].rearrange("(k p) c -> p k c", p=P)).then_inc(ple_wg_in, 16)
                    if c > 0:
                        e.wait_ge(ple_value_full, c)
                    e.dma_start(wp, flat["ple_wp"][bass.ds(l * PLE, PLE), c * PC:(c + 1) * PC].rearrange("(k p) c -> p k c", p=P)).then_inc(ple_wp_in, 16)
                end_layer(e, l)
            outr = out.rearrange("(b p) d -> p b d", p=P)
            e.dma_start(outr, x[:, :, :]).then_inc(out_done, 16)
            e.wait_ge(out_done, 16)

        @block.gpsimd
        def _(e):
            with e.Fori(0, DEPTH) as l:
                for b in range(NB):
                    e.memset(ml_v[:, b, :, AD:AD + 1], 1.0).then_inc(vones_set, 1)
                for step, i in MIXER_STEPS:
                    if step == "ret_qk":
                        if i >= 2:
                            e.wait_ge(*step_done("ret_tr", i - 2))
                        e.wait_ge(rope_terms, i + 1)
                        e.tensor_tensor(rot[i % 2], rot[i % 2], rot_b[i % 2], ALU.add).then_inc(rot_rows, 1)
                    elif step == "ret_pv" and i == H - 1:
                        e.wait_ge(*step_done("ret_pv", i))
                        for n in range(4):
                            e.memset(pads[n][:, 0:3], 0.0).then_inc(pads_clear, 1)
                    elif step == "ml_vo":
                        e.wait_ge(params_in, 80)
                        e.wait_ge(ml_o_ready, i + 1)
                        e.tensor_tensor(ml_o[:, i, :], ml_o[:, i, :], normg[:, H * DV:], ALU.mult).then_inc(ml_o_scaled, 1)
                    elif step == "ret_g":
                        e.wait_ge(ret_silu, i + 1)
                        e.tensor_tensor(ret_gate[:, i, :], ret_gate[:, i, :], normg[:, 0:H * DV], ALU.mult)
                        e.drain()
                        e.wait_ge(ret_normed, 1)
                        e.tensor_tensor(acc[:, i, 0:H * DV], acc[:, i, 0:H * DV], ret_gate[:, i, :], ALU.mult).then_inc(mix_ret, 1)

                def gather(table, ring, landed, free, h, b, ks):
                    for k in ks:
                        e.wait_ge(free, h * (NB * TOPK) + (b * TOPK + k + 1))
                        e.sem_inc(held, 1)
                        s = k % len(ring)
                        e.indirect_dma_start(ring[s], None, table, bass.IndirectOffsetOnAxis(ap=rows[:, b, k:k + 1], axis=0)).then_inc(landed[s], 16)

                U = (a["peer_u"], urow, u_in, u_free)
                V = (a["peer_v"], vrow, v_in, v_free)

                def gathers(h, first_head=False):
                    for b in range(NB):
                        e.wait_ge(chosen_rows, h * NB + (b + 1))
                        if first_head and b == 0:
                            gather(*U, h, b, range(UR))
                            gather(*V, h, b, range(VR - VLATE))
                            gather(*U, h, b, range(UR, TOPK))
                            gather(*V, h, b, range(VR - VLATE, TOPK))
                        else:
                            gather(*U, h, b, range(TOPK))
                            gather(*V, h, b, range(TOPK))

                gathers(0, first_head=True)
                with e.Fori(1, PH) as h:
                    gathers(h)
                end_layer(e, l, lead=True)

        @block.scalar
        def _(e):
            e.wait_ge(keep_in, 16)
            with e.Fori(0, DEPTH) as l:
                gw = a["gate_w"].rearrange("l r c -> (l r) c")[bass.ds(l * D, D), :]
                e.dma_start(gate_w[:, :, :], gw.rearrange("(k p) c -> p k c", p=P)).then_inc(gate_w_in, 16)
                e.dma_start(gate_b[:, :], a["gate_b"].rearrange("l h c -> (l h) c")[bass.ds(l * (FROW + H), FROW + H), :]).then_inc(gate_w_in, 16)
                e.dma_start(convw.rearrange("p g w -> p (g w)"), a["conv_w"].rearrange("l p c -> (l p) c")[bass.ds(l * P, P), :]).then_inc(gate_w_in, 16)
                def choice(b):
                    e.activation(gexp[:, b, :], gexp[:, b, :], ACT.Exp, bias=neg_best[:, b:b + 1], accum_out=gsum[:, b:b + 1]).then_inc(gexp_ready, 1)

                def gelu(n, b):
                    e.wait_ge(u_free, n * TOPK + (UR + TOPK))
                    e.activation(act_d, dots[:, b % 2, :], ACT.Gelu).then_inc(gelu_done, 1)

                def copy_first_q(i):
                    e.wait_ge(first_q_full, i + 1)
                    src = bank[4 + i % 2][:, 0:2 * P].rearrange("p (x t) -> p x t", x=2)
                    e.copy(qT[:, :, i * P:(i + 1) * P], src).then_inc(first_q_ready, 1)

                for step, i in MIXER_STEPS:
                    if step == "xt" and i % 2 == 0:
                        e.copy(xT[:, i, :], read(e, step, i)[:, :]).then_inc(freed(step, i), 1)
                        e.drain()
                        e.sem_inc(xT_ready, 1)
                    elif step == "ret_tr":
                        src = read(e, step, i).rearrange("p (g t) -> p g t", g=4)
                        e.copy(ret_qkT[:, :, i * P:(i + 1) * P], src).then_inc(freed(step, i), 1)
                        e.drain()
                        e.sem_inc(ret_qkT_ready, 1)
                    elif step == "ret_v":
                        if i == 1:
                            e.wait_ge(gate_abs, 1)
                            e.activation(gt, gt, ACT.Exp, scale=-1.0)
                            e.drain()
                            e.activation(gt, gt, ACT.Ln, bias=1.0).then_inc(gate_log, 1)
                        e.copy(ret_v[:, i, :], read(e, step, i)[:, :]).then_inc(freed(step, i), 1)
                        e.drain()
                        e.sem_inc(ret_v_ready, 1)
                    elif step == "att_qk":
                        if i == 0:
                            e.wait_ge(*step_done("ret_tr", NB - 1))
                        e.copy(att_rows4[i], read(e, step, i)[:, :]).then_inc(freed(step, i), 1)
                        e.drain()
                        e.sem_inc(att_copied, 1)
                    elif step == "att_v":
                        e.copy(att_v[:, i, :], read(e, step, i)[:, 0:256]).then_inc(freed(step, i), 1)
                        e.drain()
                        e.sem_inc(att_v_ready, 1)
                    elif step == "ret_pv":
                        src = read(e, step, i).rearrange("p (b c) -> p b c", b=NB)
                        e.copy(acc[:, :, i * DV:(i + 1) * DV], src).then_inc(freed(step, i), 1)
                        e.drain()
                        e.sem_inc(ret_raw, 1)
                    elif step == "ret_norm":
                        e.wait_ge(var_ready, 1)
                        e.sqrt(rstd[:, :], rstd[:, :]).then_inc(std_ready, 1)
                    elif step == "gate_cols":
                        e.wait_ge(gate_cols_ready, 1)
                        e.activation(gcols[:, 1, :, :], gcols[:, 1, :, :], ACT.Exp, scale=-1.0).then_inc(gate_exp, 1)
                    elif step == "ml_qk":
                        e.wait_ge(pads_clear, 4)
                        e.copy(pads[i][:, 3:], read(e, step, i)[:, :]).then_inc(freed(step, i), 1)
                        e.drain()
                        e.sem_inc(pad_filled, 1)
                        e.wait_ge(conv_done, i + 1)
                        e.activation(ml_qkT[:, i, :], ml_qkT[:, i, :], ACT.Silu).then_inc(ml_qkT_ready, 1)
                    elif step == "att_s":
                        for m, (j, _) in enumerate(sum(ROW_BANKS, ())):
                            pr = probs[i % 2][:, ROWS_AT[j]:ROWS_AT[j] + (j + 1) * P]
                            e.wait_ge(att_masked, i * NB + m + 1)
                            e.activation(pr, pr, ACT.Exp, scale=-1.0, bias=nmax[:, i, j:j + 1], accum_out=den[:, i, j:j + 1]).then_inc(att_probs, 1)
                    elif step == "ml_vo":
                        if i == 0:
                            e.wait_ge(vones_set, NB)
                        src = read(e, step, i)
                        e.copy(ml_v[:, i, :, 0:AD], src[:, 0:256].rearrange("p (h c) -> p h c", h=H))
                        e.activation(ml_o[:, i, :], src[:, 256:512], ACT.Sigmoid).then_inc(freed(step, i), 1)
                        e.drain()
                        e.sem_inc(ml_v_ready, 1)
                        e.sem_inc(ml_o_ready, 1)
                    elif step == "ml_s":
                        for m, (j, _) in enumerate(sum(TRI_BANKS, ())):
                            st = strips[i % 2][:, TRI_AT[j]:TRI_AT[j] + TRI[j]]
                            e.wait_ge(ml_expo, i * NB + m + 1)
                            e.activation(st, st, ACT.Exp, bias=gcols[:, 0, j, i:i + 1]).then_inc(ml_weight, 1)
                    elif step == "ret_g":
                        e.activation(ret_gate[:, i, :], read(e, step, i)[:, :], ACT.Silu).then_inc(freed(step, i), 1)
                        e.drain()
                        e.sem_inc(ret_silu, 1)
                    elif step == "ml_norm":
                        e.wait_ge(var_ready, 2)
                        e.sqrt(rstd[:, :], rstd[:, :]).then_inc(std_ready, 1)
                    elif (step, i) in (("out", 1), ("out", 3), ("out", 5), ("first_q", NB - 2)):
                        if step == "first_q":
                            copy_first_q(i)
                            e.wait_ge(chosen_rows, 1)
                            choice(0)
                            gelu(0, 0)
                            e.wait_ge(var_ready, 2 + NB)
                        else:
                            e.wait_ge(var_ready, 3 + i // 2)
                        e.sqrt(rstd[:, 0:1], rstd[:, 0:1]).then_inc(std_ready, 1)
                    elif step == "mix_tr":
                        src = read(e, step, i, 1).rearrange("p (k t) -> p k t", k=4)
                        e.copy(xT[:, 4:8, i * P:(i + 1) * P], src).then_inc(freed(step, i, 1), 1)
                        e.drain()
                        e.sem_inc(mixT_ready, 1)
                    elif step == "x1_tr":
                        for n in range(2):
                            src = read(e, step, i, n).rearrange("p (k t) -> p k t", k=4)
                            e.copy(xT[:, 4 * n:4 * n + 4, i * P:(i + 1) * P], src).then_inc(freed(step, i, n), 1)
                        e.drain()
                        e.sem_inc(x1T_ready, 1)
                    elif step == "first_q":
                        copy_first_q(i)

                def queries():
                    for n in range(2):
                        e.copy(qT[:, n, :], bank[4 + n][:, :])
                    e.drain()
                    e.sem_inc(q_ready, 1)

                e.wait_ge(chosen_rows, 2)
                choice(1)

                def head(h, more, first_head=False):
                    for b in range(NB):
                        n = h * NB + b
                        if b > 0 or not first_head:
                            gelu(n, b)
                        if first_head and b == 1:
                            e.wait_ge(chosen_rows, NB - 1)
                            choice(NB - 2)
                        for c in choices(b, more, first_head):
                            e.wait_ge(chosen_rows, h * NB + NB + (c + 1) % NB)
                            choice(c)
                        if b == 0 and more and not first_head:
                            e.wait_ge(q_full, h + 2)
                            queries()
                        if not more:
                            e.wait_ge(ple_gate_full, b + 1)
                            if b > 0:
                                e.wait_ge(ple_added, b)
                            for m in range(2):
                                ins = e.activation(ple_s[:, m * 512:(m + 1) * 512], bank[4 + m][:, :], ACT.Sigmoid)
                            ins.then_inc(ple_gate, 1)
                        e.wait_ge(wgt_ready, n + 1)
                        for k in range(TOPK):
                            e.wait_ge(v_free, n * TOPK + (VR + k - DR + 1))
                            e.activation(diag[:, k % DR, :], ident, ACT.Copy, scale=wgt[:, b % 2, k:k + 1]).then_inc(diag_ready, 1)
                            if not more and b == NB - 1 and k == TOPK // 2:
                                e.wait_ge(var_ready, 3 + NB)
                                e.sqrt(rstd[:, 0:NB - 1], rstd[:, 0:NB - 1]).then_inc(std_ready, 1)
                        if first_head and b == 0:
                            e.wait_ge(q_full, 2)
                            queries()
                            e.wait_ge(x1_ready, NB)
                            for c in range(NB):
                                e.mul(acc[:, c, :], x[:, c, :], ALPHA).then_inc(acc_started, 1)

                head(0, True, first_head=True)
                with e.Fori(1, PH - 1) as h:
                    head(h, True)
                head(PH - 1, False)
                e.wait_ge(var_ready, 4 + NB)
                e.sqrt(rstd[:, 0:1], rstd[:, 0:1]).then_inc(std_ready, 1)
                end_layer(e, l)

        @block.vector
        def _(e):
            e.wait_ge(keep_in, 16)

            def head_stats(c, width, h):
                for b in range(NB):
                    e.bn_stats(stats[:, h * NB + b, :], acc[:, b, c:c + width])
                e.drain()
                for b in range(NB):
                    e.bn_aggr(mv[:, h * NB + b, :], stats[:, h * NB + b, :])
                e.drain()

            def head_norm(at_col, width, count):
                e.tensor_scalar(rstd[:, :], mv[:, :, 1], EPS, None, ALU.add).then_inc(var_ready, 1)
                e.wait_ge(std_ready, count)
                e.reciprocal(rstd[:, :], rstd[:, :])
                e.drain()
                for h in range(H):
                    for b in range(NB):
                        n = h * NB + b
                        v = acc[:, b, at_col + h * width:at_col + (h + 1) * width]
                        e.tensor_scalar(v, v, mv[:, n, 0:1], rstd[:, n:n + 1], ALU.subtract, ALU.mult)

            def layer_norm(src, g, count, dst):
                w = len(src)
                for m, rows_ in enumerate(src):
                    for n in range(2):
                        e.bn_stats(stats[:, 2 * m + n, :], rows_[:, n * 512:(n + 1) * 512])
                e.drain()
                for m in range(w):
                    e.bn_aggr(mv[:, m, :], stats[:, 2 * m:2 * m + 2, :].rearrange("p n c -> p (n c)"))
                e.drain()
                e.tensor_scalar(rstd[:, 0:w], mv[:, 0:w, 1], EPS, None, ALU.add).then_inc(var_ready, 1)
                for m, rows_ in enumerate(src):
                    e.scalar_tensor_tensor(rows_, rows_, mv[:, m, 0:1], ln[:, g, :], ALU.subtract, ALU.mult)
                e.wait_ge(std_ready, count)
                e.reciprocal(rstd[:, 0:w], rstd[:, 0:w])
                e.drain()
                for m, rows_ in enumerate(src):
                    ins = e.scalar_tensor_tensor(dst[m], rows_, rstd[:, m:m + 1], ln[:, g + 1, :], ALU.mult, ALU.add)
                return ins

            e.memset(layer_row[:, :], 0.0)
            e.drain()
            with e.Fori(0, DEPTH) as l:
                def choose(b):
                    sc = bank[6 + b % 2][:, (b // 2) * 256:(b // 2) * 256 + 256].rearrange("p (x n) -> p x n", x=2)
                    for s in range(2):
                        r = rest[:, s * NKEYS:(s + 1) * NKEYS]
                        e.max(top[:, s, 0:8], sc[:, s, :])
                        e.drain()
                        e.max_index(topi[:, s, 0:8], top[:, s, 0:8], sc[:, s, :])
                        e.match_replace(r, top[:, s, 0:8], sc[:, s, :], LOWEST)
                        e.drain()
                        e.max(top[:, s, 8:16], r)
                        e.drain()
                        e.max_index(topi[:, s, 8:16], top[:, s, 8:16], r)
                    e.drain()
                    pr = pairs.rearrange("p (i j) -> p i j", i=TOPK)
                    e.tensor_tensor(pr, top[:, 0, :].unsqueeze(2).to_broadcast([P, TOPK, TOPK]),
                                    top[:, 1:2, :].to_broadcast([P, TOPK, TOPK]), ALU.add)
                    e.tensor_copy(topi_f, topi[:, :, :])
                    e.drain()
                    e.max(best[:, 0:8], pairs)
                    e.drain()
                    e.max_index(pos[:, 0:8], best[:, 0:8], pairs)
                    e.match_replace(pairs2, best[:, 0:8], pairs, LOWEST)
                    e.drain()
                    e.max(best[:, 8:16], pairs2)
                    e.drain()
                    e.max_index(pos[:, 8:16], best[:, 8:16], pairs2)
                    e.tensor_copy(gexp[:, b, :], best)
                    e.tensor_scalar(neg_best[:, b:b + 1], best[:, 0:1], -1.0, None, ALU.mult)
                    e.drain()
                    e.tensor_scalar(rank[:, 0, :], pos[:, :], 4, None, ALU.logical_shift_right)
                    e.tensor_scalar(rank[:, 1, :], pos[:, :], 15, None, ALU.bitwise_and)
                    e.drain()
                    e.tensor_copy(rank_f, rank[:, :, :])
                    e.drain()
                    oh = onehot.rearrange("p (x k r) -> p x k r", x=2, k=TOPK)
                    it = iota16.unsqueeze(1).to_broadcast([P, TOPK, TOPK])
                    for s in range(2):
                        e.tensor_tensor(oh[:, s], rank_f[:, s, :].unsqueeze(2).to_broadcast([P, TOPK, TOPK]), it, ALU.is_equal)
                    e.drain()
                    for s in range(2):
                        e.tensor_tensor(oh[:, s], oh[:, s], topi_f[:, s:s + 1, :].to_broadcast([P, TOPK, TOPK]), ALU.mult)
                    e.drain()
                    e.tensor_reduce(chosen, oh, AX_X, ALU.add)
                    e.drain()
                    e.scalar_tensor_tensor(row_f, chosen[:, 0, :], float(NKEYS), chosen[:, 1, :], ALU.mult, ALU.add)
                    e.drain()
                    e.tensor_scalar(rows[:, b, :], row_f, layer_row[:, 0:1], None, ALU.add).then_inc(chosen_rows, 1)
                    e.drain()

                def dot_products(h, b):
                    n = h * NB + b
                    for k in range(TOPK):
                        s = k % UR
                        e.wait_ge(u_in[s], (l * (PH * NB) + n) * (16 * TOPK // UR) + 16 * (k // UR + 1))
                        e.tensor_tensor_reduce(urow[s], urow[s], x[:, b, :], 1.0, 0.0, ALU.mult, ALU.add, dots[:, b % 2, k:k + 1]).then_inc(u_free, 1)
                    e.drain()

                def weights(n, b):
                    e.wait_ge(gexp_ready, n + 1)
                    e.reciprocal(grec, gsum[:, b:b + 1])
                    e.drain()
                    e.wait_ge(gelu_done, n + 1)
                    e.scalar_tensor_tensor(wgt[:, b % 2, :], act_d, grec[:, 0:1], gexp[:, b, :], ALU.mult, ALU.mult).then_inc(wgt_ready, 1)
                    e.drain()

                for step, i in MIXER_STEPS:
                    if step == "xt" and i % 2 == 1:
                        e.tensor_copy(xT[:, i, :], read(e, step, i)[:, :]).then_inc(freed(step, i), 1)
                        e.drain()
                        e.sem_inc(xT_ready, 1)
                    elif step == "gate":
                        e.wait_ge(gate_w_in, 48)
                        e.tensor_scalar(gates_if, read(e, step, i)[0:FROW + H, :], gate_b[:, 0:1], None, ALU.add).then_inc(freed(step, i), 1)
                        e.memset(gone, 1.0)
                        e.drain()
                        e.scalar_tensor_tensor(gt, gf, -1.0, gf, ALU.mult, ALU.max).then_inc(gate_abs, 1)
                    elif step == "ret_qk":
                        if i == 0:
                            e.wait_ge(tables_in, 16)
                        if i >= 2:
                            e.wait_ge(*step_done("ret_tr", i - 2))
                        src = read(e, step, i).rearrange("p (g x c) -> p g x c", g=2 * H, x=2)
                        r, rb = (t[i % 2].rearrange("p (g x c) -> p g x c", g=2 * H, x=2) for t in (rot, rot_b))
                        cos = ret_cos[:, i:i + 1, :].rearrange("p o (x c) -> p o x c", x=2).to_broadcast([P, 2 * H, 2, DK // 2])
                        e.tensor_tensor(r, src, cos, ALU.mult)
                        for half in range(2):
                            sin = ret_sin[:, i:i + 1, half * 32:half * 32 + 32].to_broadcast([P, 2 * H, DK // 2])
                            ins = e.tensor_tensor(rb[:, :, half, :], src[:, :, 1 - half, :], sin, ALU.mult)
                        ins.then_inc(freed(step, i), 1)
                        e.drain()
                        e.sem_inc(rope_terms, 1)
                    elif step == "att_qk" and i == 0:
                        e.wait_ge(gate_log, 1)
                        e.scalar_tensor_tensor(gf, gf, 0.0, gt, ALU.min, ALU.subtract)
                        e.drain()
                        e.tensor_tensor_scan(gB, gone, gf, 0.0, ALU.mult, ALU.add)
                        e.drain()
                        e.tensor_tensor(gu, gi, gB, ALU.subtract)
                        e.drain()
                        e.tensor_tensor_scan(gM, gu, gu, 0.0, ALU.max, ALU.max)
                        e.drain()
                        e.tensor_tensor(gB, gB, gM, ALU.add)
                        e.drain()
                        e.sem_inc(gates_ready, 1)
                    if step == "att_qk":
                        e.wait_ge(att_copied, i + 1)
                        rr = att_rows4[i].rearrange("p (g c) -> p g c", g=2 * H)
                        n = ROPE_HALF
                        ta, tb = (rope_a[:, s, :].rearrange("p (g c) -> p g c", g=2 * H) for s in range(2))
                        e.tensor_tensor(ta, rr[:, :, 0:2 * n], att_cos[:, i:i + 1, :].to_broadcast([P, 2 * H, 2 * n]), ALU.mult)
                        for half in range(2):
                            e.tensor_tensor(tb[:, :, half * n:half * n + n], rr[:, :, (1 - half) * n:(2 - half) * n],
                                            att_sin[:, i:i + 1, half * n:half * n + n].to_broadcast([P, 2 * H, n]), ALU.mult)
                        e.drain()
                        e.tensor_tensor(rr[:, :, 0:2 * n], ta, tb, ALU.add).then_inc(att_rotated, 1)
                        e.drain()
                    elif step == "ret_s":
                        if i >= 2:
                            e.wait_ge(*step_done("ret_pv", i - 2))
                        for n, js in enumerate(TRI_BANKS):
                            src = read(e, step, i, n)
                            for j, c in js:
                                st = strips[i % 2][:, TRI_AT[j]:TRI_AT[j] + TRI[j]]
                                ins = e.tensor_tensor(st, src[:, c:c + TRI[j]], decay[:, i, 0:TRI[j]], ALU.mult)
                            ins.then_inc(freed(step, i, n), 1)
                        e.drain()
                        e.sem_inc(ret_strip, 1)
                    elif step == "att_tr":
                        src = read(e, step, i).rearrange("p (g t) -> p g t", g=4)
                        e.tensor_copy(att_qkT[:, :, i * P:(i + 1) * P], src).then_inc(freed(step, i), 1)
                        e.drain()
                        e.sem_inc(att_qkT_ready, 1)
                    elif step == "ret_norm":
                        e.wait_ge(ret_raw, H)
                        for h in range(H):
                            head_stats(h * DV, DV, h)
                        head_norm(0, DV, 1)
                        e.drain()
                        e.sem_inc(ret_normed, 1)
                    elif step == "gate_cols":
                        src = read(e, step, i)[:, 0:2 * NB * H].rearrange("p (x b h) -> p x b h", x=2, b=NB)
                        e.tensor_copy(gcols, src).then_inc(freed(step, i), 1)
                        e.drain()
                        e.sem_inc(gate_cols_ready, 1)
                    elif step == "ml_qk":
                        e.wait_ge(pad_filled, i + 1)
                        v = ml_qkT[:, i, :]
                        e.tensor_scalar(v, pads[i][:, 0:SEQ], convw[:, i, 0:1], None, ALU.mult)
                        for w in range(1, 4):
                            e.drain()
                            e.scalar_tensor_tensor(v, pads[i][:, w:w + SEQ], convw[:, i, w:w + 1], v, ALU.mult, ALU.add)
                        e.drain()
                        e.sem_inc(conv_done, 1)
                    elif step == "att_s":
                        if i >= 2:
                            e.wait_ge(*step_done("att_tp", i - 2, len(ROW_BANKS) - 1))
                        for n, js in enumerate(ROW_BANKS):
                            src = read(e, step, i, n)
                            for m, (j, c) in enumerate(js):
                                w = (j + 1) * P
                                pr = probs[i % 2][:, ROWS_AT[j]:ROWS_AT[j] + w]
                                e.tensor_tensor_reduce(pr, src[:, c:c + w], counts[:, SEQ - w:SEQ], -AD ** -0.5, -LOWEST, ALU.add, ALU.min, nmax[:, i, j:j + 1])
                                e.drain()
                                e.sem_inc(att_masked, 1)
                            e.sem_inc(freed(step, i, n), 1)
                    elif step == "att_tp":
                        if i >= 2:
                            e.wait_ge(*step_done("att_pv", i - 2))
                        for n, js in enumerate(ROW_BANKS):
                            src = read(e, step, i, n)
                            for j, c in js:
                                w = (j + 1) * P
                                ins = e.tensor_copy(probsT[i % 2][:, ROWS_AT[j]:ROWS_AT[j] + w], src[:, c:c + w])
                            ins.then_inc(freed(step, i, n), 1)
                        e.drain()
                        e.sem_inc(att_probsT, 1)
                    elif step == "att_pv":
                        e.wait_ge(att_probs, NB * (i + 1))
                        e.reciprocal(rden, den[:, i, :])
                        e.drain()
                        src = read(e, step, i)[:, 0:NB * AD].rearrange("p (b c) -> p b c", b=NB)
                        c = H * DV + i * AD
                        e.tensor_tensor(acc[:, :, c:c + AD], src, rden.unsqueeze(2).to_broadcast([P, NB, AD]), ALU.mult).then_inc(freed(step, i), 1)
                        e.drain()
                        e.sem_inc(att_done, 1)
                    elif step == "ml_s":
                        if i >= 2:
                            e.wait_ge(*step_done("ml_pv", i - 2))
                        src = read(e, step, i, 0)
                        for j, _ in sum(TRI_BANKS, ()):
                            st = strips[i % 2][:, TRI_AT[j]:TRI_AT[j] + TRI[j]]
                            ins = e.scalar_tensor_tensor(st, src[:, j * P:SEQ], -1.0, causal[:, 0:TRI[j]], ALU.mult, ALU.add)
                            ins.then_inc(ml_expo, 1)
                        e.drain()
                        e.sem_inc(freed(step, i, 0), 1)
                        done = i * NB
                        for n, js in enumerate(TRI_BANKS):
                            src = read(e, step, i, 1 + n)
                            for j, c in js:
                                st = strips[i % 2][:, TRI_AT[j]:TRI_AT[j] + TRI[j]]
                                done += 1
                                e.wait_ge(ml_weight, done)
                                ins = e.scalar_tensor_tensor(st, src[:, c:c + TRI[j]], AD ** -0.5, st, ALU.mult, ALU.mult)
                            ins.then_inc(freed(step, i, 1 + n), 1)
                        e.drain()
                        e.sem_inc(ml_strip, 1)
                    elif step == "ml_pv":
                        src = read(e, step, i)[:, 0:NB * (AD + 1)].rearrange("p (b c) -> p b c", b=NB)
                        if i == 0:
                            e.wait_ge(gate_exp, 1)
                        e.tensor_copy(mden, src[:, :, AD])
                        e.drain()
                        e.scalar_tensor_tensor(mden, mden, -1.0, mden, ALU.mult, ALU.max)
                        e.drain()
                        e.tensor_tensor(mden, mden, gcols[:, 1, :, i], ALU.max)
                        e.drain()
                        e.reciprocal(mden, mden)
                        e.drain()
                        c = H * (DV + AD) + i * AD
                        e.tensor_tensor(acc[:, :, c:c + AD], src[:, :, 0:AD], mden.unsqueeze(2).to_broadcast([P, NB, AD]), ALU.mult).then_inc(freed(step, i), 1)
                        e.drain()
                        head_stats(c, AD, i)
                    elif step == "ml_norm":
                        c = H * (DV + AD)
                        head_norm(c, AD, 2)
                        e.drain()
                        e.wait_ge(ml_o_scaled, NB)
                        for b in range(NB):
                            e.tensor_tensor(acc[:, b, c:], acc[:, b, c:], ml_o[:, b, :], ALU.mult).then_inc(mix_ml, 1)
                    elif step == "mix_tr":
                        src = read(e, step, i, 0).rearrange("p (k t) -> p k t", k=4)
                        e.tensor_copy(xT[:, 0:4, i * P:(i + 1) * P], src).then_inc(freed(step, i, 0), 1)
                        e.drain()
                        e.sem_inc(mixT_ready, 1)
                    elif step == "out":
                        if i == 0:
                            e.wait_ge(params_in, 80)
                            e.wait_ge(x_in, 16)
                        b, half = divmod(i, 2)
                        v = x[:, b, half * 512:(half + 1) * 512]
                        e.scalar_tensor_tensor(v, v, ALPHA, read(e, step, i)[:, :], ALU.mult, ALU.add).then_inc(freed(step, i), 1)
                        if half == 1:
                            e.drain()
                            layer_norm([x[:, b, :]], 0, 3 + b, [x[:, b, :]]).then_inc(x1_ready, 1)
                            e.drain()
                    elif step == "first_q" and i < NB - 1:
                        if i == 0:
                            e.sem_inc(u_free, UR)
                        if i == 1:
                            dot_products(0, 0)
                        elif i == 2:
                            weights(0, 0)
                            dot_products(0, 1)
                        e.wait_ge(scored, i + 1)
                        choose(i)

                def add_y(n, b):
                    v = acc[:, b, :]
                    for m in range(2):
                        ins = e.tensor_tensor(v[:, m * 512:(m + 1) * 512], v[:, m * 512:(m + 1) * 512], bank[2 * (b % 2) + m][:, :], ALU.add)
                    ins.then_inc(y_added, 1)
                    e.drain()

                def head(h, more, first_head=False):
                    for b in range(1 if first_head else 0, NB):
                        n = h * NB + b
                        if b > 1 or not first_head:
                            dot_products(h, b)
                        for c in choices(b, more, first_head):
                            e.wait_ge(scored, h * NB + (NB if c == NB - 1 else 2 * NB))
                            if not (first_head and c == NB - 1):
                                e.wait_ge(v_free, n * TOPK + VR)
                            e.sem_inc(held, 1)
                            choose(c)
                        weights(n, b)
                        if first_head and b == 1:
                            e.wait_ge(acc_started, NB)
                        e.wait_ge(v_free, n * TOPK + VR)
                        add_y(n, (b + NB - 1) % NB)
                        if not more:
                            e.wait_ge(ple_gate, b + 1)
                            e.wait_ge(ple_value_full, b + 1)
                            for m in range(2):
                                v = ple_s[:, m * 512:(m + 1) * 512]
                                e.tensor_tensor(v, v, bank[6 + m][:, :], ALU.mult)
                            e.drain()
                            v = acc[:, :, b * PC:(b + 1) * PC]
                            e.tensor_tensor(v, v, ple_s.rearrange("p (b c) -> p b c", b=NB), ALU.add).then_inc(ple_added, 1)
                            e.drain()

                head(0, True, first_head=True)
                with e.Fori(1, PH - 1) as h:
                    head(h, True)
                head(PH - 1, False)
                layer_norm([acc[:, b, :] for b in range(NB - 1)], 2, 3 + NB, [x[:, b, :] for b in range(NB - 1)])
                e.wait_ge(v_free, PH * NB * TOPK + VR)
                add_y(PH * NB, NB - 1)
                layer_norm([acc[:, NB - 1, :]], 2, 4 + NB, [x[:, NB - 1, :]])
                e.drain()
                e.tensor_scalar(layer_row[:, :], layer_row[:, :], float(EXPERTS), None, ALU.add)
                e.drain()
                end_layer(e, l)

        @block.tensor
        def _(e):
            e.wait_ge(keep_in, 16)
            e.wait_ge(x_in, 16)

            def project(step, i, w):
                wt, landed, count = weight(step)
                if i == 0:
                    e.wait_ge(landed, count)
                if (step, i) == ("ret_qk", 0):
                    e.wait_ge(xT_ready, KT)
                ps = fill(e, step, i)
                for k in range(KT):
                    ins = e.matmul(ps[:, 0:w], xT[:, k, i * P:(i + 1) * P], wt[:, k, :], start=(k == 0), stop=(k == KT - 1))
                ins.then_inc(filled(step, i), 1)

            def transposes(step, i, n, srcs):
                ps = fill(e, step, i, n)
                for m, src in enumerate(srcs):
                    ins = e.transpose(ps[:, m * P:(m + 1) * P], src, ident)
                ins.then_inc(filled(step, i, n), 1)

            def half(t, g, h, lo, hi):
                r = (h % 2) * 64
                return t[r:r + 64, g + h // 2, lo:hi]

            with e.Fori(0, DEPTH) as l:
                def query():
                    for n in range(2):
                        for k in range(KT):
                            ins = e.matmul(bank[4 + n][:, :], wq[:, k, n * P:(n + 1) * P], xT[:, k, :], start=(k == 0), stop=(k == KT - 1))
                    ins.then_inc(q_full, 1)

                def score(b):
                    for s in range(2):
                        c = (b // 2) * 256 + s * NKEYS
                        ins = e.matmul(bank[6 + b % 2][:, c:c + NKEYS], qT[:, s, b * P:(b + 1) * P], keys[:, s, :], start=True, stop=True)
                    ins.then_inc(scored, 1)

                for step, i in MIXER_STEPS:
                    if step == "xt":
                        transposes(step, i, 0, [x[:, b, i * P:(i + 1) * P] for b in range(NB)])
                    elif step == "gate":
                        e.wait_ge(gate_w_in, 48)
                        ps = fill(e, step, i)
                        for k in range(KT):
                            ins = e.matmul(ps[0:FROW + H, :], gate_w[:, k, :], xT[:, k, :], start=(k == 0), stop=(k == KT - 1))
                        ins.then_inc(filled(step, i), 1)
                    elif step in ("ret_qk", "ret_v", "att_qk", "att_v", "ml_vo", "ret_g"):
                        project(step, i, GROUPS[step][1])
                    elif step == "ml_qk":
                        wt, landed, count = weight(step)
                        if i == 0:
                            e.wait_ge(landed, count)
                        ps = fill(e, step, i)
                        for k in range(KT):
                            ins = e.matmul(ps[:, :], wt[:, k, i * P:(i + 1) * P], xT[:, k, :], start=(k == 0), stop=(k == KT - 1))
                        ins.then_inc(filled(step, i), 1)
                    elif step == "ret_tr":
                        e.wait_ge(rot_rows, i + 1)
                        transposes(step, i, 0, [rot[i % 2][:, m * P:(m + 1) * P] for m in range(4)])
                    elif step == "att_tr":
                        e.wait_ge(att_rotated, i + 1)
                        transposes(step, i, 0, [att_rows4[i][:, m * P:(m + 1) * P] for m in range(4)])
                    elif step == "ret_s":
                        e.wait_ge(ret_qkT_ready, NB)
                        for n, js in enumerate(TRI_BANKS):
                            ps = fill(e, step, i, n)
                            for j, c in js:
                                ins = e.matmul(ps[:, c:c + TRI[j]], half(ret_qkT, 2, i, j * P, (j + 1) * P), half(ret_qkT, 0, i, j * P, SEQ))
                            ins.then_inc(filled(step, i, n), 1)
                    elif step == "ret_pv":
                        e.wait_ge(ret_v_ready, NB)
                        e.wait_ge(ret_strip, i + 1)
                        ps = fill(e, step, i)
                        for j in range(NB):
                            for s in range(j + 1):
                                st = strips[i % 2][:, TRI_AT[s] + (j - s) * P:TRI_AT[s] + (j - s + 1) * P]
                                ins = e.matmul(ps[:, j * DV:(j + 1) * DV], st, ret_v[:, s, i * DV:(i + 1) * DV], start=(s == 0), stop=(s == j))
                        ins.then_inc(filled(step, i), 1)
                    elif step == "gate_cols":
                        e.wait_ge(gates_ready, 1)
                        ps = fill(e, step, i)
                        for m, g in enumerate((gu, gB)):
                            for b in range(NB):
                                c = (m * NB + b) * H
                                ins = e.transpose(ps[:, c:c + H], g[:, b * P:(b + 1) * P], ident[0:H, 0:H])
                        ins.then_inc(filled(step, i), 1)
                    elif step == "att_s":
                        e.wait_ge(att_qkT_ready, NB)
                        for n, js in enumerate(ROW_BANKS):
                            ps = fill(e, step, i, n)
                            for j, c in js:
                                ins = e.matmul(ps[:, c:c + (j + 1) * P], half(att_qkT, 0, i, j * P, (j + 1) * P), half(att_qkT, 2, i, 0, (j + 1) * P))
                            ins.then_inc(filled(step, i, n), 1)
                    elif step == "att_tp":
                        done = i * NB
                        for n, js in enumerate(ROW_BANKS):
                            done += len(js)
                            e.wait_ge(att_probs, done)
                            transposes(step, i, n, [probs[i % 2][:, ROWS_AT[j] + s * P:ROWS_AT[j] + (s + 1) * P] for j, _ in js for s in range(j + 1)])
                    elif step == "att_pv":
                        e.wait_ge(att_v_ready, NB)
                        e.wait_ge(att_probsT, i + 1)
                        ps = fill(e, step, i)
                        for j in range(NB):
                            for s in range(j + 1):
                                ins = e.matmul(ps[:, j * AD:(j + 1) * AD], probsT[i % 2][:, ROWS_AT[j] + s * P:ROWS_AT[j] + (s + 1) * P],
                                               att_v[:, s, i * AD:(i + 1) * AD], start=(s == 0), stop=(s == j))
                        ins.then_inc(filled(step, i), 1)
                    elif step == "ml_s":
                        ps = fill(e, step, i, 0)
                        e.matmul(ps[:, :], pick[0:H, i, :], gM).then_inc(filled(step, i, 0), 1)
                        e.wait_ge(ml_qkT_ready, 4)
                        for n, js in enumerate(TRI_BANKS):
                            ps = fill(e, step, i, 1 + n)
                            for j, c in js:
                                ins = e.matmul(ps[:, c:c + TRI[j]], half(ml_qkT, 2, i, j * P, (j + 1) * P), half(ml_qkT, 0, i, j * P, SEQ))
                            ins.then_inc(filled(step, i, 1 + n), 1)
                    elif step == "ml_pv":
                        e.wait_ge(ml_v_ready, NB)
                        e.wait_ge(ml_strip, i + 1)
                        ps = fill(e, step, i)
                        w = AD + 1
                        for j in range(NB):
                            for s in range(j + 1):
                                st = strips[i % 2][:, TRI_AT[s] + (j - s) * P:TRI_AT[s] + (j - s + 1) * P]
                                ins = e.matmul(ps[:, j * w:(j + 1) * w], st, ml_v[:, s, i, :], start=(s == 0), stop=(s == j))
                        ins.then_inc(filled(step, i), 1)
                    elif step == "mix_tr":
                        e.wait_ge(mix_ml, i + 1)
                        e.wait_ge(mix_ret, i + 1)
                        e.wait_ge(att_done, H)
                        for n in range(2):
                            transposes(step, i, n, [acc[:, i, (4 * n + m) * P:(4 * n + m + 1) * P] for m in range(4)])
                    elif step == "out":
                        b, half = divmod(i, 2)
                        e.wait_ge(mixT_ready, 2 * b + 2)
                        ps = fill(e, step, i)
                        for k in range(KT):
                            wt, landed, count = out_weight(k // 4)
                            if i == 0 and k % 4 == 0:
                                e.wait_ge(landed, count)
                            ins = e.matmul(ps[:, :], xT[:, k, b * P:(b + 1) * P], wt[:, k % 4, half * 512:(half + 1) * 512], start=(k == 0), stop=(k == KT - 1))
                        ins.then_inc(filled(step, i), 1)
                    elif step == "x1_tr":
                        e.wait_ge(x1_ready, i + 1)
                        for n in range(2):
                            transposes(step, i, n, [x[:, i, (4 * n + m) * P:(4 * n + m + 1) * P] for m in range(4)])
                        if i == NB - 2:
                            e.drain()
                            e.sem_inc(v_free, VLATE)
                    elif step == "first_q":
                        e.wait_ge(x1T_ready, i + 1)
                        if i == 0:
                            e.sem_inc(v_free, VR - VLATE)
                            e.wait_ge(wq_in, 16)
                        if i >= 2:
                            e.wait_ge(first_q_ready, i - 1)
                        for n in range(2):
                            for k in range(KT):
                                ins = e.matmul(bank[4 + i % 2][:, n * P:(n + 1) * P], wq[:, k, n * P:(n + 1) * P], xT[:, k, i * P:(i + 1) * P], start=(k == 0), stop=(k == KT - 1))
                        ins.then_inc(first_q_full, 1)
                        if i == NB - 1:
                            e.drain()
                            e.sem_inc(q_full, 1)
                        e.wait_ge(first_q_ready, i + 1)
                        if i == 0:
                            e.wait_ge(keys_in, 16)
                        if i >= 2:
                            e.wait_ge(chosen_rows, i - 1)
                        score(i)

                def embedding_gate(c):
                    e.wait_ge(ple_wg_in, 16 * (c + 1))
                    if c == 0:
                        e.wait_ge(pT_in, 32)
                    else:
                        e.wait_ge(ple_gate, c)
                    for t in range(NB):
                        g = bank[4 + t // 2][:, (t % 2) * PC:(t % 2 + 1) * PC]
                        for k in range(KT):
                            e.matmul(g, xT[:, k, t * P:(t + 1) * P], wq[:, k, :], start=(k == 0), stop=False)
                        ins = e.matmul(g, ones[0:1, :], bg[0:1, c * PC:(c + 1) * PC], start=False, stop=True)
                    ins.then_inc(ple_gate_full, 1)

                def embedding_value(c):
                    e.wait_ge(ple_wp_in, 16 * (c + 1))
                    if c == 0:
                        e.wait_ge(chosen_rows, PH * NB)
                    else:
                        e.wait_ge(ple_added, c)
                    for t in range(NB):
                        v = bank[6 + t // 2][:, (t % 2) * PC:(t % 2 + 1) * PC]
                        for k in range(2):
                            ins = e.matmul(v, pT[:, k, t * P:(t + 1) * P], wp[:, k, :], start=(k == 0), stop=(k == 1))
                    ins.then_inc(ple_value_full, 1)

                def head(h, more, first_head=False):
                    if more and not first_head:
                        e.wait_ge(wq_in, h * 16 + 32)
                        e.wait_ge(q_ready, h)
                        query()
                    for b in range(NB):
                        n = h * NB + b
                        if not more:
                            embedding_value(b)
                        if not (first_head and b < 2):
                            e.wait_ge(y_added, h * NB + (b - 1)) if first_head or b > 0 else e.wait_ge(y_added, h * NB - 1)
                        for k in range(TOPK):
                            e.wait_ge(v_in[k], (l * (PH * NB) + n) * 16 + 16)
                            e.wait_ge(diag_ready, n * TOPK + (k + 1))
                            for m in range(2):
                                ins = e.matmul(bank[2 * (b % 2) + m][:, :], diag[:, k % DR, :], vrow[k][:, m * 512:(m + 1) * 512], start=(k == 0), stop=(k == TOPK - 1))
                            ins.then_inc(v_free, 1)
                        if not more and b < NB - 1:
                            embedding_gate(b + 1)
                        if b == 0 and first_head:
                            e.wait_ge(wq_in, 32)
                            query()
                        if b == 0 and more:
                            e.wait_ge(q_ready, h + 1)
                            e.wait_ge(keys_in, h * 16 + 32)
                            e.wait_ge(chosen_rows, h * NB + NB)
                            for c in range(NB):
                                score(c)

                head(0, True, first_head=True)
                with e.Fori(1, PH - 1) as h:
                    head(h, True)
                embedding_gate(0)
                head(PH - 1, False)
                end_layer(e, l)


def kernel(**inputs):
    import concourse.bacc as _bacc
    from concourse.bass_utils import run_bass_kernel_spmd as _run

    i = {n: np.asarray(v) for n, v in inputs.items()}
    keep, mixer = tables()
    c = np.ascontiguousarray
    gate_w, gate_b = np.zeros((DEPTH, D, FROW + H), np.float32), np.zeros((DEPTH, FROW + H, 1), np.float32)
    for n, at in enumerate((0, FROW)):
        gate_w[:, :, at:at + H] = i["w_in"][:, :, GATE_COL + n * H:GATE_COL + (n + 1) * H]
        gate_b[:, at:at + H, 0] = i["b_if"][:, n * H:(n + 1) * H]
    arrays = {
        "keep": keep,
        "mixer": mixer,
        "x": c(i["x"][0]),
        "pT": c(i["p"][:, 0].transpose(0, 2, 1)),
        "w_in": c(i["w_in"]),
        "conv_w": c(i["conv_w"].reshape(DEPTH, 4, 4, P).transpose(0, 3, 2, 1).reshape(DEPTH, P, 16)),
        "gate_w": gate_w,
        "gate_b": gate_b,
        "norm_g": c(np.concatenate([i["ret_norm_g"], i["mlstm_norm_g"]], 1)),
        "w_out": c(i["w_out"]),
        "ln": c(np.stack([i["ln1_g"], i["ln1_b"], i["ln2_g"], i["ln2_b"]], 1)),
        "peer_wq": c(i["peer_wq"]),
        "keysT": c(i["peer_keys"].transpose(0, 1, 4, 2, 3)),
        "peer_u": c(i["peer_u"].reshape(DEPTH * EXPERTS, D)),
        "peer_v": c(i["peer_v"].reshape(DEPTH * EXPERTS, D)),
        "ple_wg": c(i["ple_wg"]),
        "ple_bg": c(i["ple_bg"]),
        "ple_wp": c(i["ple_wp"]),
    }
    nc = _bacc.Bacc("TRN2", target_bir_lowering=False, num_devices=1)
    aps = {n: nc.dram_tensor(f"in_{n}", v.shape, F32, kind="ExternalInput").ap() for n, v in arrays.items()}
    out = nc.dram_tensor("out", (SEQ, D), F32, kind="ExternalOutput").ap()
    build(nc, aps, out)
    r = _run(nc, [{f"in_{n}": v for n, v in arrays.items()}], core_ids=[0])
    return r.results[0]["out"].reshape(1, SEQ, D)
```
